# Optimizing a Trainium2 kernel written in Bass

```python
import math, functools
import jax, jax.numpy as jnp
from jax import lax
import numpy as np

D_MODEL = 2048
BATCH = 1
SEQ = 256
DEPTH = 1
DEC_BATCH = 8
DEC_SEQ = 8
PAST_LEN = 2048
PAGE_SIZE = 128

MIX = D_MODEL
HEAD_DIM = 64
ATT_WIDTH = MIX // 2
N_HEADS = ATT_WIDTH // HEAD_DIM
SSM_WIDTH = MIX // 4
SSM_GROUP = 16
N_SSM_GROUPS = SSM_WIDTH // SSM_GROUP
SSM_STATE = 64
CONV_CH = MIX // 4
CONV_K = 3
ATT_PATTERNS = ((128, 1), (512, 4), (2048, 16))
ATT_SPAN = 128
ATT_BLOCK = 128
ATT_MAX_WINDOW = 2048
D_FF = -(-8 * D_MODEL // (3 * 256)) * 256
IN_COLS = 3 * ATT_WIDTH + SSM_WIDTH + 3 * CONV_CH
SPLITS = (ATT_WIDTH, 2 * ATT_WIDTH, 3 * ATT_WIDTH, 3 * ATT_WIDTH + SSM_WIDTH,
          3 * ATT_WIDTH + SSM_WIDTH + CONV_CH, 3 * ATT_WIDTH + SSM_WIDTH + 2 * CONV_CH)
DT_MIN = 0.001
DT_MAX = 0.1
RMS_EPS = 1e-6
NEG = -1e30

kernel_name = 'hymba_s5_shortconv_dilated_swa_step'

def rmsnorm(x, g):
    xf = x.astype(jnp.float32)
    y = xf * lax.rsqrt(jnp.mean(xf * xf, axis=-1, keepdims=True) + RMS_EPS)
    return (y * g.astype(jnp.float32)).astype(x.dtype)

def to_streams(t, d):
    b, s = t.shape[:2]
    t = t.reshape((b, s // d, d) + t.shape[2:])
    t = jnp.moveaxis(t, 2, 1)
    return t.reshape((b * d, s // d) + t.shape[3:])

def from_streams(t, b, d):
    n, l = t.shape[:2]
    t = t.reshape((b, d, l) + t.shape[2:])
    t = jnp.moveaxis(t, 1, 2)
    return t.reshape((b, l * d) + t.shape[3:])

def band_attention(q, k, v):
    n, l = q.shape[:2]
    nb = -(-l // ATT_BLOCK)
    lp = nb * ATT_BLOCK
    pad = ((0, 0), (0, lp - l), (0, 0), (0, 0))
    q, k, v = [jnp.pad(t, pad).reshape(n, nb, ATT_BLOCK, N_HEADS, HEAD_DIM) for t in (q, k, v)]

    def with_prev(t):
        prev = jnp.pad(t[:, :-1], ((0, 0), (1, 0), (0, 0), (0, 0), (0, 0)))
        return jnp.concatenate([prev, t], axis=2)

    kb, vb = with_prev(k), with_prev(v)
    s = jnp.einsum('nbqhd,nbkhd->nbhqk', q, kb) * (HEAD_DIM ** -0.5)
    qi = jnp.arange(ATT_BLOCK)[:, None]
    kj = jnp.arange(2 * ATT_BLOCK)[None, :]
    dist = qi + ATT_BLOCK - kj
    blk = jnp.arange(nb)[:, None, None]
    valid = (dist >= 0) & (dist <= ATT_SPAN) & ((blk > 0) | (kj >= ATT_BLOCK))
    s = jnp.where(valid[None, :, None], s, NEG)
    lse = jax.nn.logsumexp(s, axis=-1)
    p = jnp.exp(s - lse[..., None])
    o = jnp.einsum('nbhqk,nbkhd->nbqhd', p, vb).reshape(n, lp, N_HEADS, HEAD_DIM)[:, :l]
    lse = jnp.moveaxis(lse, 2, 3).reshape(n, lp, N_HEADS)[:, :l]
    return o, lse

def combine_branches(outs, lses):
    w = jax.nn.softmax(jnp.stack(lses, axis=0), axis=0)
    return jnp.einsum('pbsh,pbshd->bshd', w, jnp.stack(outs, axis=0))

def dilated_attention_prompt(q, k, v):
    b = q.shape[0]
    outs, lses = [], []
    for _, d in ATT_PATTERNS:
        o, lse = band_attention(to_streams(q, d), to_streams(k, d), to_streams(v, d))
        outs.append(from_streams(o, b, d))
        lses.append(from_streams(lse, b, d))
    return combine_branches(outs, lses)

def dilated_attention_sample(q, k, v, kv_buf):
    t = q.shape[1]
    w_buf = kv_buf.shape[1]
    k_all = jnp.concatenate([kv_buf[:, :, 0].astype(jnp.float32), k], axis=1)
    v_all = jnp.concatenate([kv_buf[:, :, 1].astype(jnp.float32), v], axis=1)
    steps = jnp.arange(ATT_SPAN + 1)
    outs, lses = [], []
    for _, d in ATT_PATTERNS:
        idx = w_buf + jnp.arange(t)[:, None] - steps[None, :] * d
        valid = idx >= 0
        idx = jnp.maximum(idx, 0)
        kg = k_all[:, idx]
        vg = v_all[:, idx]
        s = jnp.einsum('bthd,btkhd->bthk', q, kg) * (HEAD_DIM ** -0.5)
        s = jnp.where(valid[None, :, None, :], s, NEG)
        lse = jax.nn.logsumexp(s, axis=-1)
        p = jnp.exp(s - lse[..., None])
        outs.append(jnp.einsum('bthk,btkhd->bthd', p, vg))
        lses.append(lse)
    return combine_branches(outs, lses)

def ssm_mixer(u, p, h0):
    f32 = jnp.float32
    bt, l, _ = u.shape
    uf = u.astype(f32).reshape(bt, l, N_SSM_GROUPS, SSM_GROUP)
    a_re = p['ssm_a_re'].astype(f32)
    a_im = p['ssm_a_im'].astype(f32)
    dt = jnp.exp(p['ssm_log_dt'].astype(f32))[:, None]
    mag = jnp.exp(a_re * dt)
    ang = a_im * dt
    ab_re, ab_im = mag * jnp.cos(ang), mag * jnp.sin(ang)
    den = a_re * a_re + a_im * a_im
    nr, ni = ab_re - 1.0, ab_im
    cf_re = (nr * a_re + ni * a_im) / den
    cf_im = (ni * a_re - nr * a_im) / den
    b_re, b_im = p['ssm_b_re'].astype(f32), p['ssm_b_im'].astype(f32)
    bb_re = cf_re[..., None] * b_re - cf_im[..., None] * b_im
    bb_im = cf_re[..., None] * b_im + cf_im[..., None] * b_re
    x_re = jnp.einsum('blgc,gnc->blgn', uf, bb_re)
    x_im = jnp.einsum('blgc,gnc->blgn', uf, bb_im)
    a_re_b = jnp.broadcast_to(ab_re, x_re.shape)
    a_im_b = jnp.broadcast_to(ab_im, x_re.shape)

    def comb(e1, e2):
        ar1, ai1, br1, bi1 = e1
        ar2, ai2, br2, bi2 = e2
        return (ar2 * ar1 - ai2 * ai1, ar2 * ai1 + ai2 * ar1,
                ar2 * br1 - ai2 * bi1 + br2, ar2 * bi1 + ai2 * br1 + bi2)

    pr, pi, h_re, h_im = lax.associative_scan(comb, (a_re_b, a_im_b, x_re, x_im), axis=1)
    if h0 is not None:
        s_re = h0[0].astype(f32)[:, None]
        s_im = h0[1].astype(f32)[:, None]
        h_re, h_im = h_re + pr * s_re - pi * s_im, h_im + pr * s_im + pi * s_re
    c_re, c_im = p['ssm_c_re'].astype(f32), p['ssm_c_im'].astype(f32)
    y = (jnp.einsum('blgn,gcn->blgc', h_re, c_re) - jnp.einsum('blgn,gcn->blgc', h_im, c_im)
         + p['ssm_d'].astype(f32) * uf)
    y = jax.nn.gelu(y.reshape(bt, l, SSM_WIDTH))
    y = y * jax.nn.sigmoid(y @ p['ssm_w_glu'].astype(f32) + p['ssm_b_glu'].astype(f32))
    return y.astype(u.dtype), h_re[:, -1], h_im[:, -1]

def conv_mixer(h, gb, gc, w_conv, buf):
    u = gc * h
    l = u.shape[1]
    if buf is None:
        prefix = jnp.zeros((u.shape[0], CONV_K - 1, u.shape[2]), u.dtype)
    else:
        prefix = buf.astype(u.dtype)
    up = jnp.concatenate([prefix, u], axis=1)
    y = sum(w_conv[j] * up[:, j:j + l] for j in range(CONV_K))
    return gb * y, up[:, -(CONV_K - 1):]

def trunk_layer(x, p, attend, conv_buf, ssm_h0):
    bt, l, _ = x.shape
    xn = rmsnorm(x, p['g_mix_norm'])
    z = xn @ p['w_in']
    q, k, v, u, h, gb, gc = jnp.split(z, SPLITS, axis=-1)
    heads = lambda t: t.reshape(bt, l, N_HEADS, HEAD_DIM).astype(jnp.float32)
    q, k, v = heads(q), heads(k), heads(v)
    o_att = attend(q, k, v).reshape(bt, l, ATT_WIDTH).astype(x.dtype)
    y_ssm, h_re, h_im = ssm_mixer(u, p, ssm_h0)
    y_conv, conv_state = conv_mixer(h, gb, gc, p['conv_w'], conv_buf)
    g = p['g_out']
    mixed = jnp.concatenate([
        rmsnorm(o_att, g[:ATT_WIDTH]),
        rmsnorm(y_ssm.astype(x.dtype), g[ATT_WIDTH:ATT_WIDTH + SSM_WIDTH]),
        rmsnorm(y_conv.astype(x.dtype), g[ATT_WIDTH + SSM_WIDTH:])], axis=-1)
    x = x + mixed @ p['w_out']
    xn = rmsnorm(x, p['g_ffn_norm'])
    x = x + (jax.nn.silu(xn @ p['w_gate']) * (xn @ p['w_up'])) @ p['w_down']
    return x, k, v, conv_state, h_re, h_im

def setup_inputs(seed: int = 0) -> dict:
    key = jax.random.key(seed)
    ks = jax.random.split(key, 26)
    f32 = jnp.float32
    nrm = lambda k, shape, scale: scale * jax.random.normal(k, shape, f32)
    gain = lambda k, shape: 1.0 + 0.02 * jax.random.normal(k, shape, f32)
    kv_buf = min(ATT_MAX_WINDOW, PAST_LEN)
    sshape = (DEPTH, N_SSM_GROUPS, SSM_STATE)
    a_im_init = jnp.pi * jnp.arange(SSM_STATE, dtype=f32)
    return {
        'x_prompt': nrm(ks[0], (BATCH, SEQ, D_MODEL), 1.0),
        'x_sample': nrm(ks[1], (DEC_BATCH, DEC_SEQ, D_MODEL), 1.0),
        'cache_kv': nrm(ks[2], (DEPTH, DEC_BATCH, kv_buf, 2, N_HEADS, HEAD_DIM), 1.0),
        'state_conv': nrm(ks[3], (DEPTH, DEC_BATCH, CONV_K - 1, CONV_CH), 1.0),
        'state_ssm_re': nrm(ks[4], (DEPTH, DEC_BATCH, N_SSM_GROUPS, SSM_STATE), 0.5),
        'state_ssm_im': nrm(ks[5], (DEPTH, DEC_BATCH, N_SSM_GROUPS, SSM_STATE), 0.5),
        'g_mix_norm': gain(ks[6], (DEPTH, D_MODEL)),
        'w_in': nrm(ks[7], (DEPTH, D_MODEL, IN_COLS), D_MODEL ** -0.5),
        'ssm_a_re': -0.5 + nrm(ks[8], sshape, 0.01),
        'ssm_a_im': a_im_init + nrm(ks[9], sshape, 0.01),
        'ssm_log_dt': jax.random.uniform(ks[10], (DEPTH, N_SSM_GROUPS), f32, math.log(DT_MIN), math.log(DT_MAX)),
        'ssm_b_re': nrm(ks[11], (DEPTH, N_SSM_GROUPS, SSM_STATE, SSM_GROUP), (2 * SSM_GROUP) ** -0.5),
        'ssm_b_im': nrm(ks[12], (DEPTH, N_SSM_GROUPS, SSM_STATE, SSM_GROUP), (2 * SSM_GROUP) ** -0.5),
        'ssm_c_re': nrm(ks[13], (DEPTH, N_SSM_GROUPS, SSM_GROUP, SSM_STATE), (2 * SSM_STATE) ** -0.5),
        'ssm_c_im': nrm(ks[14], (DEPTH, N_SSM_GROUPS, SSM_GROUP, SSM_STATE), (2 * SSM_STATE) ** -0.5),
        'ssm_d': nrm(ks[15], (DEPTH, N_SSM_GROUPS, SSM_GROUP), 1.0),
        'ssm_w_glu': nrm(ks[16], (DEPTH, SSM_WIDTH, SSM_WIDTH), SSM_WIDTH ** -0.5),
        'ssm_b_glu': nrm(ks[17], (DEPTH, SSM_WIDTH), 0.01),
        'conv_w': nrm(ks[18], (DEPTH, CONV_K, CONV_CH), CONV_K ** -0.5),
        'g_out': gain(ks[19], (DEPTH, MIX)),
        'w_out': nrm(ks[20], (DEPTH, MIX, D_MODEL), MIX ** -0.5),
        'g_ffn_norm': gain(ks[21], (DEPTH, D_MODEL)),
        'w_gate': nrm(ks[22], (DEPTH, D_MODEL, D_FF), D_MODEL ** -0.5),
        'w_up': nrm(ks[23], (DEPTH, D_MODEL, D_FF), D_MODEL ** -0.5),
        'w_down': nrm(ks[24], (DEPTH, D_FF, D_MODEL), D_FF ** -0.5),
        'g_final': gain(ks[25], (D_MODEL,)),
    }

def reference(x_prompt, x_sample, cache_kv, state_conv, state_ssm_re, state_ssm_im,
              g_mix_norm, w_in, ssm_a_re, ssm_a_im, ssm_log_dt, ssm_b_re, ssm_b_im,
              ssm_c_re, ssm_c_im, ssm_d, ssm_w_glu, ssm_b_glu, conv_w, g_out, w_out,
              g_ffn_norm, w_gate, w_up, w_down, g_final):
    n_keep = min(ATT_MAX_WINDOW, x_prompt.shape[1])
    xp, xs = x_prompt, x_sample
    kv_p, conv_p, sre_p, sim_p = [], [], [], []
    kv_s, conv_s, sre_s, sim_s = [], [], [], []
    for i in range(DEPTH):
        p = {'g_mix_norm': g_mix_norm[i], 'w_in': w_in[i], 'ssm_a_re': ssm_a_re[i],
             'ssm_a_im': ssm_a_im[i], 'ssm_log_dt': ssm_log_dt[i], 'ssm_b_re': ssm_b_re[i],
             'ssm_b_im': ssm_b_im[i], 'ssm_c_re': ssm_c_re[i], 'ssm_c_im': ssm_c_im[i],
             'ssm_d': ssm_d[i], 'ssm_w_glu': ssm_w_glu[i], 'ssm_b_glu': ssm_b_glu[i],
             'conv_w': conv_w[i], 'g_out': g_out[i], 'w_out': w_out[i],
             'g_ffn_norm': g_ffn_norm[i], 'w_gate': w_gate[i], 'w_up': w_up[i], 'w_down': w_down[i]}
        xp, k, v, c_state, h_re, h_im = trunk_layer(xp, p, dilated_attention_prompt, None, None)
        kv_p.append(jnp.stack([k[:, -n_keep:], v[:, -n_keep:]], axis=2).astype(x_prompt.dtype))
        conv_p.append(c_state)
        sre_p.append(h_re)
        sim_p.append(h_im)
        attend = functools.partial(dilated_attention_sample, kv_buf=cache_kv[i])
        xs, k, v, c_state, h_re, h_im = trunk_layer(xs, p, attend, state_conv[i],
                                                    (state_ssm_re[i], state_ssm_im[i]))
        kv_s.append(jnp.stack([k, v], axis=2).astype(cache_kv.dtype))
        conv_s.append(c_state)
        sre_s.append(h_re)
        sim_s.append(h_im)
    y_prompt = rmsnorm(xp, g_final)
    y_sample = rmsnorm(xs, g_final)
    return (y_prompt, y_sample,
            jnp.stack(kv_p), jnp.stack(conv_p), jnp.stack(sre_p), jnp.stack(sim_p),
            jnp.stack(kv_s), jnp.stack(conv_s), jnp.stack(sre_s), jnp.stack(sim_s))


_drawn_inputs = setup_inputs


def setup_inputs(seed=0):
    import zlib

    import numpy as np

    out = dict(_drawn_inputs(seed))
    spreads = {}
    factors = {'ssm_a_re': 13.363,
     'ssm_b_glu': 21.388,
     'g_out': 3.851,
     'g_ffn_norm': 4.931,
     'g_final': 7.387}
    for name, (base, spread) in spreads.items():
        noise = np.random.default_rng([zlib.crc32(name.encode()), seed]).standard_normal(out[name].shape)
        drawn = base * np.exp(spread * noise) if base else spread * noise
        out[name] = __import__('jax').numpy.asarray(drawn.astype(out[name].dtype))
    for name, factor in factors.items():
        out[name] = (out[name] * factor).astype(out[name].dtype)
    return out
```

```python
import math
from contextlib import ExitStack

import concourse.bass as bass
import numpy as np
from concourse import mybir

ALU = mybir.AluOpType
ACT = mybir.ActivationFunctionType
AX = mybir.AxisListType
F32 = mybir.dt.float32
F32R = mybir.dt.float32r
I32 = mybir.dt.int32
ds = bass.ds

P = 128
D_MODEL, SEQ, DEC_BATCH, DEC_SEQ, PAST_LEN = 2048, 256, 8, 8, 2048
NT = SEQ + DEC_BATCH * DEC_SEQ
KT = D_MODEL // P
N_HEADS, HEAD_DIM = 16, 64
ATT_WIDTH = N_HEADS * HEAD_DIM
SSM_WIDTH = CONV_CH = 512
SSM_GROUP, SSM_STATE = 16, 64
N_GROUPS = SSM_WIDTH // SSM_GROUP
ST = N_GROUPS * SSM_STATE // P
D_FF = 5632
FT = D_FF // P
IN_COLS = 5120
ZT = IN_COLS // P
EPS = 1e-6
NEG = -1e30
SCALE = HEAD_DIM ** -0.5
PATTERNS = ((128, 1), (512, 4), (2048, 16))

ZQ, ZK, ZV, ZU, ZH, ZGB, ZGC = 0, 8, 16, 24, 28, 32, 36
NF = 8
NC = 4
SL = SEQ + DEC_BATCH * (DEC_SEQ + 1)
STEP1 = DEC_SEQ + 1
CL = (SEQ + 2) + DEC_BATCH * (DEC_SEQ + 2)

START = 1
ONE_AHEAD = """ps_masked ppt_moved po_moved x_rot y_acc sq_done
o_done po_done c_done pt_done ppt_done ssm_h""".split()

KEYS_OLD = 768
KEY_TILES = (KEYS_OLD + 512) // P
NKEYS = KEY_TILES * P + DEC_BATCH * DEC_SEQ

UNIT = 1024
RAW, SPL = 4, 2
U_IN, U_DOWN = D_MODEL // 256, D_FF // 256
N_IN = IN_COLS // 512 * U_IN
N_OUT = D_MODEL // 512 * U_IN
N_GU = 2 * D_FF // 512 * U_IN
N_DN = D_MODEL // 512 * U_DOWN


def multiplicity(dist):
    return sum(((dist >= 0) & (dist <= w) & (dist % d == 0)).astype(np.int64) for w, d in PATTERNS)


def log_mask(count):
    return np.where(count > 0, np.log(np.maximum(count, 1)) / SCALE, NEG).astype(np.float32)


def cache_positions():
    old = np.arange(PAST_LEN - 512)
    return np.concatenate([old[old % 16 < 8], np.arange(PAST_LEN - 512, PAST_LEN)])


def constants():
    t = np.arange(P) % DEC_SEQ
    past = log_mask(multiplicity(PAST_LEN + t[:, None] - cache_positions()[None, :]))
    new = np.full((P, 2 * DEC_BATCH - 1, DEC_SEQ), NEG, np.float32)
    new[:, DEC_BATCH - 1] = log_mask(multiplicity(t[:, None] - np.arange(DEC_SEQ)[None, :]))
    q = np.arange(P)[:, None]
    first = log_mask(multiplicity(q - np.arange(P)[None, :]))
    second = log_mask(multiplicity(q + P - np.arange(2 * P)[None, :]))
    keep = np.ones((P, SL), np.float32)
    keep[:, 0] = 0
    keep[:, SEQ::STEP1] = 0
    return np.concatenate([np.eye(P, dtype=np.float32), past, new.reshape(P, -1), first, second, keep], axis=1)


C_ID, C_PAST = 0, P
C_NEW = C_PAST + KEY_TILES * P
C_PROMPT = C_NEW + (2 * DEC_BATCH - 1) * DEC_SEQ
C_KEEP = C_PROMPT + 3 * P
C_END = C_KEEP + SL

V_MIX, V_OUT, V_FFN, V_FIN, V_D, V_GLU, V_CW = 0, 16, 32, 48, 64, 68, 72
V_ARE, V_AIM, V_DT = 84, 100, 116
V_END = 132


class Steps:

    def __init__(self, eng, sem):
        self.eng, self.sem, self.done, self.it, self.per = eng, sem, 0, None, 0

    def value(self):
        return self.done if self.it is None else self.it * self.per + self.done

    def __call__(self, ins, wait=True):
        ins.then_inc(self.sem, 1)
        self.done += 1
        if wait:
            self.eng.wait_ge(self.sem, self.value())

    def enter(self, it, per):
        self.it, self.per, self.start = it, per, self.done

    def leave(self, n):
        assert self.done - self.start == self.per, (self.done - self.start, self.per)
        self.done = self.start + n * self.per
        self.it = None


def build(nc, a, o):
    with ExitStack() as ctx:
        base = (nc.sbuf_base + 63) // 64 * 64
        top = [base]

        def at(name, shape, dt=F32, offset=None):
            return nc.alloc_sbuf_tensor_at(name, shape, dt, offset=base + offset)

        class Region:

            def __init__(self, start, end):
                self.pos, self.end = start, end

            def take(self, name, shape, dt=F32):
                t = at(name, shape, dt, self.pos)
                self.pos += (4 * int(np.prod(shape[1:])) + 31) // 32 * 32
                assert self.pos <= self.end, (name, self.pos, self.end)
                return t

        X0, XN0 = 5952, 5952 + 20480
        RING0 = XN0 + 40960
        H0 = RING0 + 32768
        END = H0 + 112640
        ZEND = H0 + ZT * NT * 4
        assert base + END <= nc.sbuf_usable_end

        keep = Region(0, X0)
        ident = keep.take("ident", [P, P])
        ones = keep.take("ones", [P, P])
        vec = keep.take("vec", [P, V_END])
        rstd = keep.take("rstd", [P, NT])
        rtmp = keep.take("rtmp", [P, NT])
        var = keep.take("var", [P, NT])
        halo = keep.take("halo", [P, NC, 2 * DEC_BATCH])

        x1 = at("x1", [P, KT, NT], F32, X0)
        xh = at("xh", [P, KT, NT], F32R, XN0)
        xl = at("xl", [P, KT, NT], F32R, XN0 + KT * NT * 4)
        xm = at("xm", [P, KT, NT], F32, XN0 + KT * NT * 4)
        yout = at("yout", [P, KT, NT], F32, XN0)
        ring = Region(RING0, H0)
        raw = ring.take("raw", [P, RAW, UNIT])
        whi = ring.take("whi", [P, SPL, UNIT], F32R)
        wlo = ring.take("wlo", [P, SPL, UNIT], F32R)
        hh = at("hh", [P, FT, NT], F32R, H0)
        hl = at("hl", [P, FT, NT], F32R, H0 + FT * NT * 4)
        hm = at("hm", [P, FT, NT], F32, H0 + FT * NT * 4)
        z = at("z", [P, ZT, NT], F32, H0)
        upper = Region(ZEND, END)
        vt = upper.take("vt", [P, KEY_TILES, ATT_WIDTH])
        kt = upper.take("kt", [P, 4, NF * P])
        bt = upper.take("bt", [P, 2, NC, P])
        sq = at("sq", [P, 2, 4, NT], F32, ZEND)
        deadv = Region(H0 + ZV * NT * 4, H0 + ZU * NT * 4)
        ptk = deadv.take("ptk", [P, KEY_TILES + 1, P])
        qbd = deadv.take("qbd", [P, DEC_BATCH, NF, 2 * DEC_SEQ])
        deadg = Region(H0 + ZGB * NT * 4, ZEND)
        sp = deadg.take("sp", [P, 2, 3 * P])
        ptp = deadg.take("ptp", [P, 3 * P])
        qs = deadg.take("qs", [P, SEQ])
        ks = deadg.take("ks", [P, SEQ])
        vs = deadg.take("vs", [P, 2, P])
        low = Region(XN0, H0)
        const = low.take("const", [P, C_END - P])
        sall = low.take("sall", [P, 2, NKEYS])
        sk = low.take("sk", [P, 2, 4 * P])
        vp = low.take("vp", [P, 2, ATT_WIDTH])
        vn = low.take("vn", [P, ATT_WIDTH])
        cmat = low.take("cmat", [P, 2, ST, 32])
        h0 = low.take("h0", [P, 2, ST, DEC_BATCH])
        ho = low.take("ho", [P, 2, ST, STEP1])
        par = low.take("par", [P, 30, ST])
        pari = low.take("pari", [P, 2, ST], I32)
        smax = low.take("smax", [P, 4, 2])
        pmax = low.take("pmax", [P, 4, 4])
        us = low.take("us", [P, SL])
        bs = low.take("bs", [P, 2, P])
        cs = low.take("cs", [P, 2, 4, 32])
        dcol = low.take("dcol", [P, 1])
        magc = low.take("magc", [P, 1])
        SSM0 = low.pos
        tabc = low.take("tabc", [P, 2, SL])
        tabs = low.take("tabs", [P, 2, SL])
        dec = low.take("dec", [P, 2, SL])
        xr = low.take("xr", [P, 2, SL])
        gr = low.take("gr", [P, 2, SL])
        tm = low.take("tm", [P, 4, SL])
        hb = low.take("hb", [P, 2, 2, SL])
        ptmp = low.take("ptmp", [P, 4, P])
        early = Region(SSM0, H0)
        cu = early.take("cu", [P, NC, CL])
        ca = early.take("ca", [P, NC, CL])
        bmat = early.take("bmat", [P, 2, ST, 32])
        btmp = early.take("btmp", [P, 4, ST, 32])
        late = Region(SSM0, H0)
        wglu = late.take("wglu", [P, NC, SSM_WIDTH])
        ysig = late.take("ysig", [P, NC, NT])

        ps = ctx.enter_context(nc.psum_tensor("ps", [P, 8, 512], F32))

        names = """x_in const_in vec_in ssm_in glu_in kv_stored conv_stored stored
        ones_set sq_ready sq_used var_ready root_ready rstd_step rstd_ready m_ready m_hi m_lo
        w_hi w_lo unit_done free0 free1 h_hi h_lo y_ready y_step
        vpt_done vp_moved conv_done statics_zero par_step par_exp bt_ready bt_done bt_moved
        sin_ready sin_done qbd_ready pool_step dve_step
        k_used v_used sk_moved sq_done s_masked s_max p_exp p_norm pt_done pt_moved o_done o_moved
        q_static ps_done ps_masked ps_max pp_exp pp_norm ppt_done ppt_moved po_done po_moved
        ssm_static tab_ready x_proj x_rot ssm_h c_done y_acc y_glu glu_done glu_sig mixed_done""".split()
        names += [f"raw_in{i}" for i in range(RAW)] + [f"k_in{i}" for i in range(4)]
        names += [f"v_in{i}" for i in range(KEY_TILES)]
        S = {n: ctx.enter_context(nc.semaphore(n)) for n in names}
        RAW_IN = [S[f"raw_in{i}"] for i in range(RAW)]
        K_IN = [S[f"k_in{i}"] for i in range(4)]
        V_IN = [S[f"v_in{i}"] for i in range(KEY_TILES)]
        FREE = [S["free0"], S["free1"]]

        GEMMS = {"in": (a["w_in"], 0, IN_COLS // 1024, U_IN, 0),
                 "out": (a["w_out"], N_IN, 2, U_IN, 5),
                 "gu": (a["w_gu"], N_IN + N_OUT, D_FF // 512, U_IN, 7),
                 "dn": (a["w_dn"], N_IN + N_OUT + N_GU, 2, U_DOWN, 18)}
        PAIRS = 20

        NORMS = [(0, KT, V_MIX), (0, 8, V_OUT), (8, 4, V_OUT + 8), (12, 4, V_OUT + 12), (0, KT, V_FFN), (0, KT, V_FIN)]

        def tiles_before(k):
            return sum(n for _, n, _ in NORMS[:k])

        def norm_source(k, i, n=1):
            if k in (0, 4, 5):
                return x1[:, i:i + n, :]
            first = {1: ZQ, 2: ZU, 3: ZH}[k]
            return z[:, first + i:first + i + n, :]

        score_turn = {}
        for r in range(2):
            for key in [("s", r, g) for g in range(3)] + [("p", r, e) for e in range(2)]:
                score_turn[key] = len(score_turn)
        turn = {}
        for r in range(2):
            for key in [("sq", r, g) for g in range(3)] + [("pt", r, g) for g in range(3)] + [("pp", r, e) for e in range(2)]:
                turn[key] = len(turn)

        def score_bank(*key):
            return score_turn[key] % 2

        def turn_bank(*key):
            return 2 + turn[key] % 2

        block = ctx.enter_context(nc.Block())

        @block.sync
        def _(sy):
            def weights(which):
                src, first, pairs, units, _ = GEMMS[which]
                with sy.Fori(0, pairs) as it:
                    for j in range(2 * units):
                        sy.wait_ge(S["w_lo"], it * (2 * units) + (first + j + 1))
                        sy.dma_start(raw[:, j % RAW, :], src[ds(it * (2 * units) + j, 1), :, :].rearrange("a p n -> p (a n)")) \
                            .then_inc(RAW_IN[j % RAW], 16)

            sy.dma_start(vec[:], a["vecs"]).then_inc(S["vec_in"], 16)
            for c in range(4):
                sy.dma_start(x1[:, 4 * c:4 * c + 4, :], a["xt"][:, 4 * c:4 * c + 4, :]).then_inc(S["x_in"], 16)
                sy.wait_ge(S["x_in"], 16 * (c + 1))
            sy.dma_start(ident[:], a["consts"][:, 0:P]).then_inc(S["const_in"], 16)
            sy.dma_start(halo[:], a["halo"]).then_inc(S["const_in"], 16)
            weights("in")

            def load_k(n, j):
                sy.wait_ge(S["k_used"], n + (j + 1))
                sy.dma_start(kt[:, j % 4, :], a["ck"][ds(n + j, 1), :, :].rearrange("a p n -> p (a n)")).then_inc(K_IN[j % 4], 16)

            def load_v(n, j):
                sy.wait_ge(S["v_used"], n + (j + 1))
                slot = j % KEY_TILES
                sy.dma_start(vt[:, slot, :], a["cv"][ds(n + j, 1), :, :].rearrange("a p n -> p (a n)")).then_inc(V_IN[slot], 16)

            sy.wait_ge(S["sq_used"], KT)
            for j in range(4):
                load_k(0, j)
            for j in range(KEY_TILES):
                load_v(0, j)
            sy.wait_ge(S["unit_done"], SPL + N_IN)
            sy.dma_start(bmat[:], a["ssm_b"]).then_inc(S["ssm_in"], 16)
            sy.dma_start(cmat[:], a["ssm_c"]).then_inc(S["ssm_in"], 16)
            sy.dma_start(h0[:], a["state"]).then_inc(S["ssm_in"], 16)
            sy.dma_start(const[:], a["consts"][:, P:C_END]).then_inc(S["const_in"], 16)
            for g in range(2):
                sy.wait_ge(FREE[g], 1 + IN_COLS // 1024)
            sy.dma_start(o["kv"], z[:, ZK:ZU, :]).then_inc(S["kv_stored"], 16)
            sy.wait_ge(S["conv_done"], 1)
            sy.dma_start(o["conv"][:, :, 0:2], cu[:, :, SEQ:SEQ + 2]).then_inc(S["conv_stored"], 16)
            for c in range(NC):
                sy.dma_start(o["conv"][:, c, 2:18].rearrange("p (b j) -> p b j", j=2),
                             cu[:, c, SEQ + 2:CL].rearrange("p (b s) -> p b s", s=DEC_SEQ + 2)[:, :, DEC_SEQ:]) \
                    .then_inc(S["conv_stored"], 16)

            def cache(it, last):
                n = it * (2 * KEY_TILES)
                for r in range(2):
                    for j in range(KEY_TILES * r + 4, KEY_TILES * (r + 1) + (0 if last and r else 4)):
                        load_k(n, j)
                    if not (last and r):
                        for j in range(KEY_TILES * (r + 1), KEY_TILES * (r + 2)):
                            load_v(n, j)

            with sy.Fori(0, NC - 1) as it:
                cache(it, False)
            cache(NC - 1, True)
            sy.wait_ge(S["y_acc"], NC + START)
            sy.dma_start(wglu[:], a["w_glu"]).then_inc(S["glu_in"], 16)
            sy.dma_start(o["state"], ho[:]).then_inc(S["glu_in"], 16)
            sy.wait_ge(S["mixed_done"], 1)
            weights("out")
            weights("gu")
            weights("dn")
            for c in range(4):
                sy.wait_ge(S["y_ready"], 4 * (c + 1))
                sy.dma_start(o["y"][:, 4 * c:4 * c + 4, :], yout[:, 4 * c:4 * c + 4, :]).then_inc(S["stored"], 16)
            sy.wait_ge(S["kv_stored"], 16)
            sy.wait_ge(S["conv_stored"], 16 * (1 + NC))
            sy.wait_ge(S["glu_in"], 32)
            sy.wait_ge(S["stored"], 64)

        @block.scalar
        def _(act):
            def square(k):
                for c in range(NORMS[k][1] // 4):
                    q = tiles_before(k) // 4 + c
                    if k == 0:
                        act.wait_ge(S["x_in"], 16 * (c + 1))
                    if q >= 2:
                        act.wait_ge(S["sq_used"], 4 * (q - 1))
                    act.activation(sq[:, q % 2], norm_source(k, 4 * c, 4), ACT.Square).then_inc(S["sq_ready"], 1)

            def root(k):
                act.wait_ge(S["var_ready"], k + 1)
                act.activation(rtmp[:], var[:], ACT.Sqrt).then_inc(S["root_ready"], 1)

            def high(k):
                first, n, _ = NORMS[k]
                for i in range(n):
                    act.wait_ge(S["m_ready"], tiles_before(k) + i + 1)
                    act.activation(xh[:, first + i, :], xm[:, first + i, :], ACT.Copy).then_inc(S["m_hi"], 1)

            def split(which, it, j):
                _, first, _, units, _ = GEMMS[which]
                act.wait_ge(RAW_IN[j % RAW], it * (16 * 2 * units // RAW) + 16 * ((first + j) // RAW + 1))
                act.wait_ge(S["unit_done"], it * (2 * units) + (first + j + 1))
                act.activation(whi[:, j % SPL, :], raw[:, j % RAW, :], ACT.Copy).then_inc(S["w_hi"], 1)

            square(0)
            root(0)
            high(0)

            def z_out(it, g):
                act.wait_ge(S["unit_done"], it * (2 * U_IN) + (SPL + U_IN * (g + 1)))
                act.activation(z[:, ds(it * 8 + 4 * g, 4), :], ps[:, 4 * g:4 * g + 4, 0:NT], ACT.Copy).then_inc(FREE[g], 1)

            def z_pair(it, first):
                for j in range(2 * U_IN):
                    split("in", it, j)
                    if j == 1 and not first:
                        z_out(it - 1, 1)
                    if j == U_IN + 1:
                        z_out(it, 0)

            z_pair(0, True)
            with act.Fori(1, IN_COLS // 1024) as it:
                z_pair(it, False)
            z_out(IN_COLS // 1024 - 1, 1)

            act.wait_ge(S["sin_ready"], 2)
            act.activation(par[:, 14:16, :], par[:, 12:14, :], ACT.Sin).then_inc(S["sin_done"], 1)
            for c in range(6):
                act.wait_ge(S["vpt_done"], c + 1)
                dst = vp[:, c // 2, 512 * (c % 2):512 * (c % 2) + 512] if c < 4 else vn[0:64, 512 * (c - 4):512 * (c - 3)]
                act.activation(dst, ps[0:(P if c < 4 else 64), c, :], ACT.Copy).then_inc(S["vp_moved"], 1)

            with act.Fori(0, NC) as it:
                for r in range(2):
                    for g in range(3):
                        k = 3 * r + g
                        w = 512 if g < 2 else 256
                        act.wait_ge(S["k_used"], it * (2 * KEY_TILES) + (4 + KEY_TILES * r + min(4 * (g + 1), KEY_TILES)))
                        act.wait_ge(S["sq_done"], it * 6 + max(k - 1, 0) + START)
                        b = score_bank("s", r, g)
                        act.activation(sk[:, k % 2, 0:w], ps[:, b, 0:w], ACT.Copy).then_inc(S["sk_moved"], 1)
                        if g == 2:
                            act.activation(sk[0:64, k % 2, 256:384], ps[0:64, b, 256:384], ACT.Copy).then_inc(S["sk_moved"], 1)
                    act.wait_ge(S["s_max"], it * 2 + (r + 1))
                    act.activation(sall[:, r], sall[:, r], ACT.Exp, bias=smax[:, 1, r:r + 1], scale=SCALE,
                                   accum_out=smax[:, 2, r:r + 1]).then_inc(S["p_exp"], 1)
                    for e in range(2):
                        for t in range(2):
                            act.wait_ge(S["ps_max"], it * 4 + (2 * r + e + 1))
                            lo, hi = (0, P) if t == 0 else (P, 3 * P)
                            act.activation(sp[:, e, lo:hi], sp[:, e, lo:hi], ACT.Exp, bias=pmax[:, 1, 2 * e + t:2 * e + t + 1],
                                           scale=SCALE, accum_out=pmax[:, 2, 2 * e + t:2 * e + t + 1]).then_inc(S["pp_exp"], 1)
                    for g in range(3):
                        act.wait_ge(S["pt_done"], it * 6 + (3 * r + g + 1) + START)
                        if g == 0:
                            act.wait_ge(S["o_done"], it * 2 + r + START)
                        b = turn_bank("pt", r, g)
                        w = 4 if g < 2 else 2
                        act.activation(ptk[:, 4 * g:4 * g + w, :].rearrange("p a n -> p (a n)"), ps[:, b, 0:w * P], ACT.Copy) \
                            .then_inc(S["pt_moved"], 1)
                        if g == 2:
                            act.activation(ptk[0:64, KEY_TILES, :], ps[0:64, b, 256:384], ACT.Copy).then_inc(S["pt_moved"], 1)
                    for e in range(2):
                        act.wait_ge(S["ppt_done"], it * 4 + (2 * r + e + 1) + START)
                        act.wait_ge(S["po_done"], it * 4 + (2 * r + e) + START)
                        act.activation(ptp[:], ps[:, turn_bank("pp", r, e), 0:3 * P], ACT.Copy).then_inc(S["ppt_moved"], 1)
                    act.wait_ge(S["po_done"], it * 4 + (2 * r + 2) + START)
                    act.activation(z[:, ds(it * 2 + r, 1), 0:SEQ].rearrange("p a n -> p (a n)"), ps[:, 4, 0:SEQ], ACT.Copy) \
                        .then_inc(S["po_moved"], 1)

            act.wait_ge(S["y_acc"], NC + START)
            for c in range(NC):
                act.activation(z[:, ZU + c, :], z[:, ZU + c, :], ACT.Gelu_apprx_tanh).then_inc(S["y_glu"], 1)
            for c in range(NC):
                act.wait_ge(S["glu_done"], c + 1)
                act.activation(ysig[:, c, :], ps[:, c, 0:NT], ACT.Sigmoid, bias=vec[:, V_GLU + c:V_GLU + c + 1]) \
                    .then_inc(S["glu_sig"], 1)
            act.wait_ge(S["mixed_done"], 1)
            for k in (1, 2, 3):
                square(k)
                root(k)
                high(k)

            def only_split(which):
                with act.Fori(0, GEMMS[which][2]) as it:
                    for j in range(2 * GEMMS[which][3]):
                        split(which, it, j)

            only_split("out")
            for g in range(2):
                act.wait_ge(FREE[g], 1 + 7)
            square(4)
            root(4)
            high(4)

            def silu(it):
                act.wait_ge(S["unit_done"], it * (2 * U_IN) + (SPL + N_IN + N_OUT + U_IN))
                act.activation(hm[:, ds(it * 4, 4), :], ps[:, 0:4, 0:NT], ACT.Silu).then_inc(FREE[0], 1)

            def h_high(it):
                act.wait_ge(FREE[1], it + (1 + 7 + 1))
                act.activation(hh[:, ds(it * 4, 4), :], hm[:, ds(it * 4, 4), :], ACT.Copy).then_inc(S["h_hi"], 1)

            def gu_pair(it, first):
                for j in range(2 * U_IN):
                    split("gu", it, j)
                    if j == 3 and not first:
                        h_high(it - 1)
                    if j == U_IN + 1:
                        silu(it)

            gu_pair(0, True)
            with act.Fori(1, D_FF // 512) as it:
                gu_pair(it, False)
            h_high(D_FF // 512 - 1)
            only_split("dn")
            for g in range(2):
                act.wait_ge(FREE[g], 1 + PAIRS)
            square(5)
            root(5)

        @block.vector
        def _(dve):
            v = nc.vector
            dve.sem_inc(S["w_lo"], RAW)
            v.memset(ones[:], 1.0).then_inc(S["ones_set"], 1)
            rstd_step = Steps(dve, S["rstd_step"])

            def norm_low(k, i):
                first = NORMS[k][0]
                dve.wait_ge(S["m_hi"], tiles_before(k) + i + 1)
                v.tensor_tensor(xl[:, first + i, :], xm[:, first + i, :], xh[:, first + i, :].bitcast(F32), ALU.subtract) \
                    .then_inc(S["m_lo"], 1)

            def norm(k):
                first, n, gain = NORMS[k]
                dve.wait_ge(S["sq_used"], tiles_before(k + 1))
                v.tensor_scalar(var[:], ps[:, 7, 0:NT], 1.0 / (P * n), EPS, ALU.mult, ALU.add).then_inc(S["var_ready"], 1)
                dve.wait_ge(S["root_ready"], k + 1)
                rstd_step(v.reciprocal(rstd[:], rtmp[:]))
                rstd_step(v.tensor_tensor(rtmp[:], rstd[:], rstd[:], ALU.mult))
                rstd_step(v.tensor_tensor(rtmp[:], rtmp[:], var[:], ALU.mult))
                rstd_step(v.tensor_scalar(rtmp[:], rtmp[:], -0.5, 1.5, ALU.mult, ALU.add))
                v.tensor_tensor(rstd[:], rstd[:], rtmp[:], ALU.mult).then_inc(S["rstd_ready"], 1)
                dve.wait_ge(S["rstd_ready"], k + 1)
                for i in range(n):
                    dst, done = (yout[:, i, :], S["y_ready"]) if k == 5 else (xm[:, first + i, :], S["m_ready"])
                    v.scalar_tensor_tensor(out=dst, in0=norm_source(k, i)[:, 0, :], scalar=vec[:, gain + i:gain + i + 1],
                                           in1=rstd[:], op0=ALU.mult, op1=ALU.mult).then_inc(done, 1)
                    if k < 5 and i:
                        norm_low(k, i - 1)
                if k < 5:
                    norm_low(k, n - 1)

            def split(which, it, j):
                _, first, _, units, _ = GEMMS[which]
                dve.wait_ge(S["w_hi"], it * (2 * units) + (first + j + 1))
                v.tensor_tensor(wlo[:, j % SPL, :], raw[:, j % RAW, :], whi[:, j % SPL, :].bitcast(F32), ALU.subtract) \
                    .then_inc(S["w_lo"], 1)

            dve.wait_ge(S["vec_in"], 16)
            norm(0)
            with dve.Fori(0, IN_COLS // 1024) as it:
                for j in range(2 * U_IN):
                    split("in", it, j)

            step = Steps(dve, S["par_step"])
            are, aim, ldt = (vec[:, c:c + ST] for c in (V_ARE, V_AIM, V_DT))

            def arr(i):
                return par[:, i, :]

            def round_to(out, x, scale):
                step(v.tensor_scalar(out, x, scale, 12582912.0, ALU.mult, ALU.add))
                step(v.tensor_scalar(out, out, -12582912.0, None, ALU.add))

            def exp(out, x, k, r):
                step(v.tensor_scalar(r, x, 88.0, -87.0, ALU.min, ALU.max))
                round_to(k, r, math.log2(math.e))
                step(v.scalar_tensor_tensor(out=r, in0=k, scalar=-0.693359375, in1=r, op0=ALU.mult, op1=ALU.add))
                step(v.scalar_tensor_tensor(out=r, in0=k, scalar=2.12194440e-4, in1=r, op0=ALU.mult, op1=ALU.add))
                step(v.tensor_scalar(out, r, 1.0 / math.factorial(8), None, ALU.mult))
                for n in range(7, 0, -1):
                    step(v.scalar_tensor_tensor(out=out, in0=out, scalar=1.0 / math.factorial(n), in1=r, op0=ALU.add, op1=ALU.mult))
                step(v.tensor_scalar(out, out, 1.0, None, ALU.add))
                step(v.tensor_scalar(k, k, 127.0, 1.0, ALU.add, ALU.max))
                step(v.tensor_copy(pari[:, 0, :], k))
                step(v.tensor_scalar(pari[:, 1, :], pari[:, 0, :], 23, None, ALU.logical_shift_left))
                step(v.tensor_tensor(out, out, pari[:, 1, :].bitcast(F32), ALU.mult))

            dve.wait_ge(S["unit_done"], SPL + N_IN)
            DT, MAG, ANG = 0, 1, 2
            exp(arr(DT), ldt, arr(3), arr(4))
            step(v.tensor_tensor(arr(5), are, arr(DT), ALU.mult))
            exp(arr(MAG), arr(5), arr(3), arr(4))
            step(v.tensor_tensor(arr(ANG), aim, arr(DT), ALU.mult))
            round_to(arr(3), arr(ANG), 1.0 / (2 * math.pi))
            turns = [6.28125, 0.0019350051879882812, 3.019916050e-07]
            step(v.scalar_tensor_tensor(out=arr(4), in0=arr(3), scalar=-turns[0], in1=arr(ANG), op0=ALU.mult, op1=ALU.add))
            for part in turns[1:]:
                step(v.scalar_tensor_tensor(out=arr(4), in0=arr(3), scalar=-part, in1=arr(4), op0=ALU.mult, op1=ALU.add))
            v.tensor_scalar(arr(12), arr(4), 3.1415925, -3.1415925, ALU.min, ALU.max).then_inc(S["sin_ready"], 1)
            dve.wait_ge(S["sin_ready"], 1)
            step(v.tensor_scalar(arr(5), arr(12), -1.0, None, ALU.mult))
            step(v.tensor_tensor(arr(5), arr(5), arr(12), ALU.max))
            v.tensor_scalar(arr(13), arr(5), -1.0, math.pi / 2, ALU.mult, ALU.add).then_inc(S["sin_ready"], 1)
            dve.wait_ge(S["sin_done"], 1)
            SIN, COS = 14, 15
            step(v.tensor_tensor(arr(5), arr(COS), arr(COS), ALU.mult))
            step(v.tensor_tensor(arr(6), arr(SIN), arr(SIN), ALU.mult))
            step(v.tensor_tensor(arr(5), arr(5), arr(6), ALU.add))
            step(v.tensor_scalar(arr(5), arr(5), -0.5, 1.5, ALU.mult, ALU.add))
            step(v.tensor_tensor(arr(COS), arr(COS), arr(5), ALU.mult))
            step(v.tensor_tensor(arr(SIN), arr(SIN), arr(5), ALU.mult))
            step(v.tensor_tensor(arr(7), arr(MAG), arr(COS), ALU.mult))
            step(v.tensor_scalar(arr(7), arr(7), -1.0, None, ALU.add))
            step(v.tensor_tensor(arr(8), arr(MAG), arr(SIN), ALU.mult))
            step(v.tensor_tensor(arr(3), are, are, ALU.mult))
            step(v.tensor_tensor(arr(4), aim, aim, ALU.mult))
            step(v.tensor_tensor(arr(3), arr(3), arr(4), ALU.add))
            step(v.reciprocal(arr(4), arr(3)))
            step(v.tensor_tensor(arr(5), arr(7), are, ALU.mult))
            step(v.tensor_tensor(arr(6), arr(8), aim, ALU.mult))
            step(v.tensor_tensor(arr(5), arr(5), arr(6), ALU.add))
            step(v.tensor_tensor(arr(9), arr(5), arr(4), ALU.mult))
            step(v.tensor_tensor(arr(5), arr(8), are, ALU.mult))
            step(v.tensor_tensor(arr(6), arr(7), aim, ALU.mult))
            step(v.tensor_tensor(arr(5), arr(5), arr(6), ALU.subtract))
            step(v.tensor_tensor(arr(10), arr(5), arr(4), ALU.mult))
            dve.wait_ge(S["ssm_in"], 48)

            def cf(i):
                return par[:, i, :].rearrange("p (s a) -> p s a", a=1).to_broadcast([P, ST, 32])

            step(v.tensor_tensor(btmp[:, 0], bmat[:, 0], cf(9), ALU.mult))
            step(v.tensor_tensor(btmp[:, 1], bmat[:, 1], cf(10), ALU.mult))
            step(v.tensor_tensor(btmp[:, 2], bmat[:, 1], cf(9), ALU.mult))
            step(v.tensor_tensor(btmp[:, 3], bmat[:, 0], cf(10), ALU.mult))
            v.tensor_tensor(bmat[:, 0], btmp[:, 0], btmp[:, 1], ALU.subtract).then_inc(S["bt_ready"], 1)
            v.tensor_tensor(bmat[:, 1], btmp[:, 2], btmp[:, 3], ALU.add).then_inc(S["bt_ready"], 1)
            step(v.tensor_scalar(cmat[:, 1], cmat[:, 1], -1.0, None, ALU.mult))

            for g in range(2):
                dve.wait_ge(FREE[g], 1 + IN_COLS // 1024)
            dve.wait_ge(S["const_in"], 48)
            sam = cu[:, :, SEQ + 2:CL].rearrange("p c (b s) -> p c b s", s=DEC_SEQ + 2)
            zs = lambda t: z[:, t:t + NC, SEQ:NT].rearrange("p c (b s) -> p c b s", s=DEC_SEQ)
            step(v.memset(cu[:, :, 0:2], 0.0), wait=False)
            step(v.tensor_tensor(cu[:, :, 2:SEQ + 2], z[:, ZGC:ZGC + NC, 0:SEQ], z[:, ZH:ZH + NC, 0:SEQ], ALU.mult), wait=False)
            step(v.tensor_copy(sam[:, :, :, 0:2], halo[:].rearrange("p c (b j) -> p c b j", j=2)), wait=False)
            for c in range(NC):
                step(v.tensor_tensor(sam[:, c, :, 2:], zs(ZGC)[:, c], zs(ZH)[:, c], ALU.mult))
            n = CL - 2
            for c in range(NC):
                cw = lambda j: vec[:, V_CW + 4 * j + c:V_CW + 4 * j + c + 1]
                step(v.tensor_scalar(ca[:, c, 0:n], cu[:, c, 0:n], cw(0), None, ALU.mult))
                for j in (1, 2):
                    step(v.scalar_tensor_tensor(out=ca[:, c, 0:n], in0=cu[:, c, j:n + j], scalar=cw(j), in1=ca[:, c, 0:n],
                                                op0=ALU.mult, op1=ALU.add))
            cas = ca[:, :, SEQ + 2:CL].rearrange("p c (b s) -> p c b s", s=DEC_SEQ + 2)
            step(v.tensor_tensor(z[:, ZH:ZH + NC, 0:SEQ], z[:, ZGB:ZGB + NC, 0:SEQ], ca[:, :, 0:SEQ], ALU.mult), wait=False)
            for c in range(NC):
                last = v.tensor_tensor(zs(ZH)[:, c], zs(ZGB)[:, c], cas[:, c, :, 0:DEC_SEQ], ALU.mult)
                if c < NC - 1:
                    step(last)
            last.then_inc(S["conv_done"], 1)
            dve.wait_ge(S["bt_done"], 2)
            for i in range(2):
                v.tensor_copy(bt[:, i].rearrange("p c n -> p (c n)"), ps[:, 6 + i, :]).then_inc(S["bt_moved"], 1)
            dve.wait_ge(S["conv_stored"], 16 * (1 + NC))

            with dve.Fori(0, NC) as it:
                step = Steps(dve, S["dve_step"])
                step.enter(it, 75)

                def scan(i):
                    b = i % 2
                    c_, s_ = tabc[:, b, :], tabs[:, b, :]
                    dve.wait_ge(S["tab_ready"], it * 4 + (i + 1))
                    dve.wait_ge(S["x_proj"], it * 4 + (i + 1))
                    xre, xim = ps[:, 6, 0:SL], ps[:, 7, 0:SL]
                    step(v.tensor_tensor(tm[:, 0], xre, c_, ALU.mult), wait=False)
                    step(v.tensor_tensor(tm[:, 1], xim, s_, ALU.mult), wait=False)
                    step(v.tensor_tensor(tm[:, 2], xim, c_, ALU.mult))
                    v.tensor_tensor(tm[:, 3], xre, s_, ALU.mult).then_inc(S["x_rot"], 1)
                    step(v.tensor_tensor(xr[:, 0], tm[:, 0], tm[:, 1], ALU.add))
                    dve.wait_ge(S["x_rot"], it * 4 + (i + 1) + START)
                    step(v.tensor_tensor(xr[:, 1], tm[:, 2], tm[:, 3], ALU.subtract))
                    step(v.tensor_copy(xr[:, :, SEQ:SL:STEP1].rearrange("p a (c b) -> p a c b", c=1),
                                       h0[:, :, ds(it * 4 + i, 1), :]))
                    for a_ in range(2):
                        step(v.tensor_tensor_scan(gr[:, a_, :], dec[:, b, :], xr[:, a_, :], 0.0, ALU.mult, ALU.add), wait=a_ == 1)
                    step(v.tensor_tensor(tm[:, 0], gr[:, 0], c_, ALU.mult), wait=False)
                    step(v.tensor_tensor(tm[:, 1], gr[:, 1], s_, ALU.mult), wait=False)
                    step(v.tensor_tensor(tm[:, 2], gr[:, 0], s_, ALU.mult), wait=False)
                    step(v.tensor_tensor(tm[:, 3], gr[:, 1], c_, ALU.mult))
                    dve.wait_ge(S["c_done"], it * 4 + max(i - 1, 0) + START)
                    step(v.tensor_tensor(hb[:, b, 0], tm[:, 0], tm[:, 1], ALU.subtract))
                    v.tensor_tensor(hb[:, b, 1], tm[:, 2], tm[:, 3], ALU.add).then_inc(S["ssm_h"], 1)
                    dve.wait_ge(S["ssm_h"], it * 4 + (i + 1) + START)
                    step(v.tensor_copy(ho[:, :, ds(it * 4 + i, 1), :],
                                       hb[:, b, :, SEQ - 1:SL:STEP1].rearrange("p a (c k) -> p a c k", c=1)))

                for r in range(2):
                    dve.wait_ge(S["pt_done"], it * 6 + START)
                    for g in range(3):
                        dve.wait_ge(S["sq_done"], it * 6 + (3 * r + g + 1) + START)
                        b = turn_bank("sq", r, g)
                        w = 512 if g < 2 else 256
                        c0 = C_PAST - P + 512 * g
                        v.tensor_tensor(sall[:, r, 512 * g:512 * g + w], ps[:, b, 0:w], const[:, c0:c0 + w], ALU.add) \
                            .then_inc(S["s_masked"], 1)
                    new = C_NEW - P + 8 * (DEC_BATCH - 1 - r)
                    v.tensor_tensor(sall[:, r, KEY_TILES * P:NKEYS], ps[:, b, 256:320], const[:, ds(it * -16 + new, 64)], ALU.add) \
                        .then_inc(S["s_masked"], 1)
                    dve.wait_ge(S["s_masked"], it * 8 + (4 * r + 4))
                    step(v.tensor_reduce(smax[:, 0, r:r + 1], sall[:, r], AX.X, ALU.max))
                    v.tensor_scalar(smax[:, 1, r:r + 1], smax[:, 0, r:r + 1], -SCALE, None, ALU.mult).then_inc(S["s_max"], 1)
                    for e in range(2):
                        dve.wait_ge(S["ps_done"], it * 4 + (2 * r + e + 1))
                        if e == 0:
                            dve.wait_ge(S["ppt_done"], it * 4 + 2 * r + START)
                        v.tensor_tensor(sp[:, e], ps[:, score_bank("p", r, e), 0:3 * P], const[:, C_PROMPT - P:C_PROMPT + 2 * P], ALU.add) \
                            .then_inc(S["ps_masked"], 1)
                        dve.wait_ge(S["ps_masked"], it * 4 + (2 * r + e + 1) + START)
                        step(v.tensor_reduce(pmax[:, 0, 2 * e:2 * e + 1], sp[:, e, 0:P], AX.X, ALU.max), wait=False)
                        step(v.tensor_reduce(pmax[:, 0, 2 * e + 1:2 * e + 2], sp[:, e, P:3 * P], AX.X, ALU.max))
                        v.tensor_scalar(pmax[:, 1, 2 * e:2 * e + 2], pmax[:, 0, 2 * e:2 * e + 2], -SCALE, None, ALU.mult) \
                            .then_inc(S["ps_max"], 1)
                    dve.wait_ge(S["p_exp"], it * 2 + (r + 1))
                    step(v.reciprocal(smax[:, 3, r:r + 1], smax[:, 2, r:r + 1]))
                    v.tensor_scalar(sall[:, r], sall[:, r], smax[:, 3, r:r + 1], None, ALU.mult).then_inc(S["p_norm"], 1)
                    dve.wait_ge(S["pp_exp"], it * 8 + (4 * r + 4))
                    step(v.reciprocal(pmax[:, 3, :], pmax[:, 2, :]))
                    for e in range(2):
                        step(v.tensor_scalar(sp[:, e, 0:P], sp[:, e, 0:P], pmax[:, 3, 2 * e:2 * e + 1], None, ALU.mult), wait=False)
                        v.tensor_scalar(sp[:, e, P:3 * P], sp[:, e, P:3 * P], pmax[:, 3, 2 * e + 1:2 * e + 2], None, ALU.mult) \
                            .then_inc(S["pp_norm"], 1)
                    scan(2 * r)
                    dve.wait_ge(S["o_done"], it * 2 + (r + 1) + START)
                    for e in range(2):
                        src = ps[64 * e:64 * e + 64, 4, 0:P].rearrange("p (f n) -> p f n", f=NF)[:, :, 8 * e:8 * e + 8]
                        v.tensor_copy(z[64 * e:64 * e + 64, 0:NF, ds(it * 16 + (SEQ + 8 * r), 8)], src).then_inc(S["o_moved"], 1)
                    scan(2 * r + 1)
                dve.wait_ge(S["c_done"], it * 4 + 4 + START)
                yb = z[:, ds(it + ZU, 1), :].rearrange("p a n -> p (a n)")
                step(v.scalar_tensor_tensor(out=yb[:, 0:SEQ], in0=us[:, 0:SEQ], scalar=dcol[:], in1=ps[:, 5, 0:SEQ],
                                            op0=ALU.mult, op1=ALU.add), wait=False)
                tail = lambda x: x.rearrange("p (b s) -> p b s", s=STEP1)[:, :, 1:]
                v.scalar_tensor_tensor(out=yb[:, SEQ:NT].rearrange("p (b s) -> p b s", s=DEC_SEQ), in0=tail(us[:, SEQ:SL]),
                                       scalar=dcol[:], in1=tail(ps[:, 5, SEQ:SL]), op0=ALU.mult, op1=ALU.add).then_inc(S["y_acc"], 1)
                step.leave(NC)

            for c in range(NC):
                dve.wait_ge(S["glu_sig"], c + 1)
                if c == 0:
                    dve.wait_ge(S["glu_done"], NC)
                if c == NC - 1:
                    dve.wait_ge(S["glu_in"], 32)
                    dve.wait_ge(S["po_moved"], 2 * NC + START)
                v.tensor_tensor(z[:, ZU + c, :], z[:, ZU + c, :], ysig[:, c, :], ALU.mult) \
                    .then_inc(S["y_step"] if c < NC - 1 else S["mixed_done"], 1)
            dve.wait_ge(S["y_step"], NC - 1)
            dve.wait_ge(S["mixed_done"], 1)
            for k in (1, 2, 3):
                norm(k)

            def x_out(which, it, g):
                _, first, _, units, _ = GEMMS[which]
                dve.wait_ge(S["unit_done"], it * (2 * units) + (SPL + first + units * (g + 1)))
                t = x1[:, ds(it * 8 + 4 * g, 4), :]
                v.tensor_tensor(t, ps[:, 4 * g:4 * g + 4, 0:NT], t, ALU.add).then_inc(FREE[g], 1)

            def x_pair(which, it, first):
                units = GEMMS[which][3]
                for j in range(2 * units):
                    split(which, it, j)
                    if j == 1 and not first:
                        x_out(which, it - 1, 1)
                    if j == units + 1:
                        x_out(which, it, 0)

            x_pair("out", 0, True)
            x_pair("out", 1, False)
            x_out("out", 1, 1)
            for g in range(2):
                dve.wait_ge(FREE[g], 1 + 7)
            norm(4)

            def gate(it):
                dve.wait_ge(FREE[0], it + (1 + 7 + 1))
                dve.wait_ge(S["unit_done"], it * (2 * U_IN) + (SPL + N_IN + N_OUT + 2 * U_IN))
                t = hm[:, ds(it * 4, 4), :]
                v.tensor_tensor(t, ps[:, 4:8, 0:NT], t, ALU.mult).then_inc(FREE[1], 1)

            def h_low(it):
                dve.wait_ge(S["h_hi"], it + 1)
                v.tensor_tensor(hl[:, ds(it * 4, 4), :], hm[:, ds(it * 4, 4), :], hh[:, ds(it * 4, 4), :].bitcast(F32), ALU.subtract) \
                    .then_inc(S["h_lo"], 1)

            def gu_pair(it, first):
                for j in range(2 * U_IN):
                    split("gu", it, j)
                    if j == 1 and not first:
                        gate(it - 1)
                    if j == 5 and not first:
                        h_low(it - 1)

            gu_pair(0, True)
            with dve.Fori(1, D_FF // 512) as it:
                gu_pair(it, False)
            gate(D_FF // 512 - 1)
            h_low(D_FF // 512 - 1)
            x_pair("dn", 0, True)
            x_pair("dn", 1, False)
            x_out("dn", 1, 1)
            for g in range(2):
                dve.wait_ge(FREE[g], 1 + PAIRS)
            norm(5)

        @block.gpsimd
        def _(pool):
            g_ = nc.gpsimd
            step = Steps(pool, S["pool_step"])
            pool.wait_ge(S["vp_moved"], 6)
            pool.wait_ge(S["kv_stored"], 16)
            step(g_.memset(qbd[:], 0.0))
            for e in range(2):
                for b in range(DEC_BATCH):
                    g_.tensor_copy(qbd[64 * e:64 * e + 64, b, :, 8 * e:8 * e + 8],
                                   z[64 * e:64 * e + 64, ZQ:ZQ + NF, SEQ + 8 * b:SEQ + 8 * b + 8]).then_inc(S["qbd_ready"], 1)
                pool.wait_ge(S["qbd_ready"], DEC_BATCH * (e + 1))
            step(g_.memset(us[:], 0.0))
            pool.wait_ge(S["bt_moved"], 2)
            pool.wait_ge(S["conv_stored"], 16 * (1 + NC))
            before = step.done
            with pool.Fori(0, NC) as it:
                step = Steps(pool, S["pool_step"])
                step.done = before
                step.enter(it, 252)

                def apart():
                    pool.wait_ge(S["kv_stored"], 16)

                def heads(r):
                    pool.wait_ge(S["po_done"], it * 4 + 2 * r + START)
                    apart()
                    for dst, t in ((qs, ZQ), (ks, ZK)):
                        step(g_.tensor_copy(dst[:].rearrange("p (a n) -> p a n", a=1), z[:, ds(it * 2 + (t + r), 1), 0:SEQ]), wait=False)
                    g_.tensor_copy(vs[:], vp[:, :, ds(it * (2 * P) + r * P, P)]).then_inc(S["q_static"], 1)

                def table(i):
                    b = i % 2
                    pool.wait_ge(S["ssm_h"], it * 4 + max(i - 1, 0) + START)
                    apart()
                    c_, s_ = tabc[:, b, :], tabs[:, b, :]
                    column = lambda k: par[:, k, ds(it * 4 + i, 1)]
                    step(g_.tensor_copy(c_[:, 0:1], column(15)), wait=False)
                    step(g_.tensor_copy(s_[:, 0:1], column(14)), wait=False)
                    step(g_.tensor_copy(magc[:], column(1)))
                    k = 1
                    while k < SEQ:
                        ck_, sk_ = (x[:, k - 1:k].to_broadcast([P, k]) for x in (c_, s_))
                        step(g_.tensor_tensor(ptmp[:, 0, 0:k], c_[:, 0:k], ck_, ALU.mult), wait=False)
                        step(g_.tensor_tensor(ptmp[:, 1, 0:k], s_[:, 0:k], sk_, ALU.mult), wait=False)
                        step(g_.tensor_tensor(ptmp[:, 2, 0:k], c_[:, 0:k], sk_, ALU.mult), wait=False)
                        step(g_.tensor_tensor(ptmp[:, 3, 0:k], s_[:, 0:k], ck_, ALU.mult))
                        step(g_.tensor_tensor(c_[:, k:2 * k], ptmp[:, 0, 0:k], ptmp[:, 1, 0:k], ALU.subtract), wait=False)
                        step(g_.tensor_tensor(s_[:, k:2 * k], ptmp[:, 2, 0:k], ptmp[:, 3, 0:k], ALU.add))
                        k *= 2
                    q0, q1 = (ptmp[:, 2 * j:2 * j + 2, :].rearrange("p a n -> p (a n)") for j in range(2))
                    step(g_.tensor_tensor(q0, c_[:, 0:SEQ], c_[:, 0:SEQ], ALU.mult), wait=False)
                    step(g_.tensor_tensor(q1, s_[:, 0:SEQ], s_[:, 0:SEQ], ALU.mult))
                    step(g_.tensor_tensor(q0, q0, q1, ALU.add))
                    step(g_.tensor_tensor(dec[:, b, :], const[:, C_KEEP - P:C_END - P], magc[:].to_broadcast([P, SL]), ALU.mult), wait=False)
                    step(g_.tensor_scalar(q0, q0, -0.5, 1.5, ALU.mult, ALU.add))
                    for x, one in ((c_, 1.0), (s_, 0.0)):
                        slots = x[:, SEQ:SL].rearrange("p (b s) -> p b s", s=STEP1)
                        first, scale = (y[:, 0:DEC_SEQ].rearrange("p (a s) -> p a s", a=1).to_broadcast([P, DEC_BATCH, DEC_SEQ])
                                        for y in (x, q0))
                        step(g_.tensor_tensor(slots[:, :, 1:], first, scale, ALU.mult), wait=False)
                        step(g_.memset(slots[:, :, 0:1], one), wait=one == 0.0)
                    step(g_.tensor_tensor(c_[:, 0:SEQ], c_[:, 0:SEQ], q0, ALU.mult), wait=False)
                    last = g_.tensor_tensor(s_[:, 0:SEQ], s_[:, 0:SEQ], q0, ALU.mult)
                    last.then_inc(S["tab_ready"], 1)

                pool.wait_ge(S["y_acc"], it + START)
                apart()
                ub = z[:, ds(it + ZU, 1), :].rearrange("p a n -> p (a n)")
                step(g_.tensor_copy(us[:, 0:SEQ], ub[:, 0:SEQ]), wait=False)
                step(g_.tensor_copy(us[:, SEQ:SL].rearrange("p (b s) -> p b s", s=STEP1)[:, :, 1:],
                                    ub[:, SEQ:NT].rearrange("p (b s) -> p b s", s=DEC_SEQ)), wait=False)
                step(g_.tensor_copy(bs[:].rearrange("p a (c n) -> p a c n", c=1), bt[:, :, ds(it, 1), :]), wait=False)
                step(g_.tensor_copy(dcol[:], vec[:, ds(it + V_D, 1)]), wait=False)
                g_.tensor_copy(cs[:], cmat[:, :, ds(it * 4, 4), :]).then_inc(S["ssm_static"], 1)
                heads(0)
                table(0)
                table(1)
                heads(1)
                table(2)
                table(3)
                step.leave(NC)

        @block.tensor
        def _(pe):
            t_ = nc.tensor
            pe.sem_inc(S["unit_done"], SPL)
            pe.sem_inc(S["free0"], 1)
            pe.sem_inc(S["free1"], 1)
            pe.sem_inc(S["k_used"], 4)
            pe.sem_inc(S["v_used"], KEY_TILES)
            for name in ONE_AHEAD:
                pe.sem_inc(S[name], START)

            def sum_squares(k):
                for c in range(NORMS[k][1] // 4):
                    q = tiles_before(k) // 4 + c
                    pe.wait_ge(S["sq_ready"], q + 1)
                    for i in range(4):
                        t_.matmul(ps[:, 7, 0:NT], ones[:], sq[:, q % 2, i, :], start=(c == 0 and i == 0),
                                  stop=(4 * c + i == NORMS[k][1] - 1)).then_inc(S["sq_used"], 1)

            def product(which, ah, al, ready):
                _, first, pairs, units, before = GEMMS[which]
                with pe.Fori(0, pairs) as it:
                    for g in range(2):
                        pe.wait_ge(FREE[g], it + (before + 1))
                        for j in range(units):
                            pe.wait_ge(S["w_lo"], it * (2 * units) + (RAW + first + g * units + j + 1))
                            slot = (g * units + j) % SPL
                            for kk in range(2):
                                k = 2 * j + kk
                                if ready and g == 0:
                                    ready(k)
                                for n in range(4):
                                    out = ps[:, 4 * g + n, 0:NT]
                                    w = slice(512 * kk + P * n, 512 * kk + P * n + P)
                                    t_.matmul(out, whi[:, slot, w], ah[:, k, :], start=(k == 0), stop=False)
                                    t_.matmul(out, whi[:, slot, w], al[:, k, :], start=False, stop=False)
                                    last = t_.matmul(out, wlo[:, slot, w], ah[:, k, :], start=False, stop=(k == 2 * units - 1))
                            last.then_inc(S["unit_done"], 1)

            pe.wait_ge(S["ones_set"], 1)
            sum_squares(0)
            product("in", xh, xl, lambda k: pe.wait_ge(S["m_lo"], k + 1))

            for g in range(2):
                pe.wait_ge(FREE[g], 1 + IN_COLS // 1024)
            pe.wait_ge(S["const_in"], 48)
            for c in range(6):
                cols = slice(P * (c // 2), P * (c // 2) + P) if c < 4 else slice(SEQ, NT)
                for i in range(4):
                    f = 4 * (c % 2) + i
                    last = t_.transpose(ps[0:(P if c < 4 else 64), c, P * i:P * i + P], z[:, ZV + f, cols], ident[:])
                last.then_inc(S["vpt_done"], 1)
            pe.wait_ge(S["bt_ready"], 2)
            for i in range(2):
                for c in range(NC):
                    last = t_.transpose(ps[:, 6 + i, P * c:P * c + P], bmat[:, i, 4 * c:4 * c + 4, :].rearrange("p s n -> p (s n)"), ident[:])
                last.then_inc(S["bt_done"], 1)
            pe.wait_ge(S["bt_moved"], 2)
            pe.wait_ge(S["vp_moved"], 6)
            pe.wait_ge(S["qbd_ready"], 2 * DEC_BATCH)

            with pe.Fori(0, NC) as it:
                def score_free(key):
                    n = score_turn[key] - 2
                    if n < 0:
                        pe.wait_ge(S["ps_masked"], it * 4 + START)
                        return
                    kind, r, g = next(k for k, m in score_turn.items() if m == n)
                    if kind == "s":
                        pe.wait_ge(S["sk_moved"], it * 8 + (4 * r + (g + 1 if g < 2 else 4)))
                    else:
                        pe.wait_ge(S["ps_masked"], it * 4 + (2 * r + g + 1) + START)

                def turn_free(key):
                    n = turn[key] - 2
                    if n < 0:
                        pe.wait_ge(S["ppt_moved"], it * 4 + START)
                        return
                    kind, r, g = next(k for k, m in turn.items() if m == n)
                    if kind == "sq":
                        pe.wait_ge(S["s_masked"], it * 8 + (4 * r + (g + 1 if g < 2 else 4)))
                    elif kind == "pt":
                        pe.wait_ge(S["pt_moved"], it * 8 + (4 * r + (g + 1 if g < 2 else 4)))
                    else:
                        pe.wait_ge(S["ppt_moved"], it * 4 + (2 * r + g + 1) + START)

                def scores(r, g):
                    score_free(("s", r, g))
                    b = score_bank("s", r, g)
                    q = lambda f: qbd[:, ds(it * 2 + r, 1), f, :].rearrange("p a n -> p (a n)")
                    for j in range(4 * g, min(4 * g + 4, KEY_TILES)):
                        n = KEY_TILES * r + j
                        pe.wait_ge(K_IN[n % 4], it * (16 * 2 * KEY_TILES // 4) + 16 * (n // 4 + 1))
                        for f in range(NF):
                            col = P * (j - 4 * g) + 16 * f
                            last = t_.matmul(ps[:, b, col:col + 16], kt[:, n % 4, P * f:P * f + P], q(f), start=True, stop=True)
                        last.then_inc(S["k_used"], 1)
                        if j == KEY_TILES - 2:
                            for f in range(NF):
                                t_.matmul(ps[0:64, b, 256 + 16 * f:272 + 16 * f], z[:, ZK + f, SEQ:NT], q(f), start=True, stop=True)

                def turn_scores(r, g):
                    turn_free(("sq", r, g))
                    b, k = turn_bank("sq", r, g), (3 * r + g) % 2
                    pe.wait_ge(S["sk_moved"], it * 8 + (4 * r + (g + 1 if g < 2 else 4)))
                    for i in range(4 if g < 2 else 2):
                        last = t_.transpose(ps[:, b, P * i:P * i + P], sk[:, k, P * i:P * i + P], ident[:])
                    if g == 2:
                        last = t_.transpose(ps[:, b, 256:320], sk[0:64, k, 256:384], ident[0:64, 0:64])
                    last.then_inc(S["sq_done"], 1)

                def prompt_scores(r):
                    pe.wait_ge(S["q_static"], it * 2 + (r + 1))
                    for e in range(2):
                        score_free(("p", r, e))
                        b, h = score_bank("p", r, e), slice(64 * e, 64 * e + 64)
                        t_.matmul(ps[:, b, 0:P], qs[h, 0:P], ks[h, 0:P], start=True, stop=True)
                        t_.matmul(ps[:, b, P:3 * P], qs[h, P:2 * P], ks[h, :], start=True, stop=True).then_inc(S["ps_done"], 1)

                def probabilities(r):
                    pe.wait_ge(S["p_norm"], it * 2 + (r + 1))
                    for g in range(3):
                        turn_free(("pt", r, g))
                        b = turn_bank("pt", r, g)
                        for i in range(4 if g < 2 else 2):
                            n = 4 * g + i
                            last = t_.transpose(ps[:, b, P * i:P * i + P], sall[:, r, P * n:P * n + P], ident[:])
                        if g == 2:
                            last = t_.transpose(ps[0:64, b, 256:384], sall[:, r, KEY_TILES * P:NKEYS], ident[:])
                        last.then_inc(S["pt_done"], 1)
                    pe.wait_ge(S["po_moved"], it * 2 + r + START)
                    for j in range(KEY_TILES + 1):
                        pe.wait_ge(S["pt_moved"], it * 8 + (4 * r + (j // 4 + 1 if j < KEY_TILES else 4)))
                        if j < KEY_TILES:
                            pe.wait_ge(V_IN[j], it * 32 + 16 * (r + 1))
                        for f in range(NF):
                            w = slice(P * f, P * f + P)
                            lhs, rhs = (vt[:, j, w], ptk[:, j, 16 * f:16 * f + 16]) if j < KEY_TILES else \
                                (vn[0:64, w], ptk[0:64, j, 16 * f:16 * f + 16])
                            last = t_.matmul(ps[:, 4, 16 * f:16 * f + 16], lhs, rhs, start=(j == 0 and f == 0),
                                             stop=(j == KEY_TILES), skip_group_check=True)
                        last.then_inc(S["v_used"] if j < KEY_TILES else S["o_done"], 1)

                def prompt_probabilities(r):
                    for e in range(2):
                        pe.wait_ge(S["pp_norm"], it * 4 + (2 * r + e + 1))
                        turn_free(("pp", r, e))
                        b = turn_bank("pp", r, e)
                        for i in range(3):
                            last = t_.transpose(ps[:, b, P * i:P * i + P], sp[:, e, P * i:P * i + P], ident[:])
                        last.then_inc(S["ppt_done"], 1)
                        if e == 0:
                            pe.wait_ge(S["o_moved"], it * 4 + (2 * r + 2))
                        pe.wait_ge(S["ppt_moved"], it * 4 + (2 * r + e + 1) + START)
                        h = slice(64 * e, 64 * e + 64)
                        t_.matmul(ps[h, 4, 0:P], vs[:, 0, h], ptp[:, 0:P], start=True, stop=True)
                        t_.matmul(ps[h, 4, P:SEQ], vs[:, 0, h], ptp[:, P:SEQ], start=True, stop=False)
                        t_.matmul(ps[h, 4, P:SEQ], vs[:, 1, h], ptp[:, SEQ:3 * P], start=False, stop=True) \
                            .then_inc(S["po_done"], 1)

                def project(i):
                    if i == 0:
                        pe.wait_ge(S["ssm_static"], it + 1)
                    pe.wait_ge(S["x_rot"], it * 4 + i + START)
                    q = slice(32 * i, 32 * i + 32)
                    t_.matmul(ps[:, 6, 0:SL], bs[q, 0, :], us[q, :], start=True, stop=True, tile_position=(32 * i, 0))
                    t_.matmul(ps[:, 7, 0:SL], bs[q, 1, :], us[q, :], start=True, stop=True, tile_position=(32 * i, 0)).then_inc(S["x_proj"], 1)

                def read_out(i):
                    pe.wait_ge(S["ssm_h"], it * 4 + (i + 1) + START)
                    if i == 0:
                        pe.wait_ge(S["y_acc"], it + START)
                    q = slice(32 * i, 32 * i + 32)
                    t_.matmul(ps[q, 5, 0:SL], cs[:, 0, i, :], hb[:, i % 2, 0], start=True, stop=False)
                    t_.matmul(ps[q, 5, 0:SL], cs[:, 1, i, :], hb[:, i % 2, 1], start=False, stop=True).then_inc(S["c_done"], 1)

                for r in range(2):
                    project(2 * r)
                    scores(r, 0)
                    scores(r, 1)
                    turn_scores(r, 0)
                    scores(r, 2)
                    turn_scores(r, 1)
                    turn_scores(r, 2)
                    if r:
                        read_out(1)
                    prompt_scores(r)
                    probabilities(r)
                    project(2 * r + 1)
                    prompt_probabilities(r)
                    read_out(2 * r)
                read_out(3)

            pe.wait_ge(S["glu_in"], 32)
            pe.wait_ge(S["y_glu"], NC)
            for n in range(NC):
                for k in range(NC):
                    last = t_.matmul(ps[:, n, 0:NT], wglu[:, k, P * n:P * n + P], z[:, ZU + k, :], start=(k == 0), stop=(k == NC - 1))
                last.then_inc(S["glu_done"], 1)
            for k in (1, 2, 3):
                if k > 1:
                    pe.wait_ge(S["var_ready"], k)
                sum_squares(k)
            pe.wait_ge(S["var_ready"], 4)
            product("out", xh, xl, lambda k: pe.wait_ge(S["m_lo"], KT + k + 1))
            for g in range(2):
                pe.wait_ge(FREE[g], 1 + 7)
            sum_squares(4)
            pe.wait_ge(S["var_ready"], 5)
            product("gu", xh, xl, lambda k: pe.wait_ge(S["m_lo"], 2 * KT + k + 1))
            pe.wait_ge(S["h_lo"], D_FF // 512)
            product("dn", hh, hl, None)
            for g in range(2):
                pe.wait_ge(FREE[g], 1 + PAIRS)
            sum_squares(5)


def pack_weights(w):
    k, n = w.shape
    return np.ascontiguousarray(w.reshape(k // 256, 2, P, n // 512, 512).transpose(3, 0, 2, 1, 4)).reshape(-1, P, UNIT)


def features(x):
    return x.reshape(x.shape[0], -1, P).transpose(2, 1, 0)


def kernel(x_prompt, x_sample, cache_kv, state_conv, state_ssm_re, state_ssm_im, g_mix_norm, w_in, ssm_a_re, ssm_a_im,
           ssm_log_dt, ssm_b_re, ssm_b_im, ssm_c_re, ssm_c_im, ssm_d, ssm_w_glu, ssm_b_glu, conv_w, g_out, w_out,
           g_ffn_norm, w_gate, w_up, w_down, g_final):
    import concourse.bacc as bacc
    from concourse.bass_utils import run_bass_kernel_spmd

    arr = np.asarray
    ins = {}
    ins["xt"] = np.concatenate([features(arr(x_prompt)[0]), features(arr(x_sample).reshape(-1, D_MODEL))], axis=2)
    pos = cache_positions()
    kv = arr(cache_kv)[0]
    ck = kv[:, pos, 0].reshape(DEC_BATCH, KEY_TILES, P, NF, P)
    ins["ck"] = ck.transpose(0, 1, 4, 3, 2).reshape(-1, P, NF * P)
    ins["cv"] = kv[:, pos, 1].reshape(-1, P, ATT_WIDTH)
    ins["w_in"] = pack_weights(arr(w_in)[0])
    ins["w_out"] = pack_weights(arr(w_out)[0])
    gate, up = pack_weights(arr(w_gate)[0]), pack_weights(arr(w_up)[0])
    ins["w_gu"] = np.stack([x.reshape(-1, U_IN, P, UNIT) for x in (gate, up)], axis=1).reshape(-1, P, UNIT)
    ins["w_dn"] = pack_weights(arr(w_down)[0])
    col = lambda x: arr(x).reshape(-1, P).T
    states = lambda x: arr(x).reshape(ST, P).T
    dt = np.repeat(arr(ssm_log_dt)[0], SSM_STATE)
    ins["vecs"] = np.concatenate([col(g_mix_norm), col(g_out), col(g_ffn_norm), col(g_final), col(ssm_d), col(ssm_b_glu),
                                  col(conv_w), states(ssm_a_re), states(ssm_a_im), states(dt)], axis=1)
    ins["halo"] = features(arr(state_conv)[0].reshape(-1, CONV_CH))
    ins["state"] = np.stack([arr(x)[0].reshape(DEC_BATCH, ST, P).transpose(2, 1, 0) for x in (state_ssm_re, state_ssm_im)], axis=1)

    def blocks(x):
        x = x.reshape(ST, 2, SSM_STATE, SSM_GROUP)
        out = np.zeros((ST, 2, SSM_STATE, 2, SSM_GROUP), x.dtype)
        out[:, 0, :, 0], out[:, 1, :, 1] = x[:, 0], x[:, 1]
        return out.reshape(ST, P, 32).transpose(1, 0, 2)

    ins["ssm_b"] = np.stack([blocks(arr(x)[0]) for x in (ssm_b_re, ssm_b_im)], axis=1)
    ins["ssm_c"] = np.stack([blocks(arr(x)[0].transpose(0, 2, 1)) for x in (ssm_c_re, ssm_c_im)], axis=1)
    ins["w_glu"] = arr(ssm_w_glu)[0].reshape(NC, P, SSM_WIDTH).transpose(1, 0, 2)
    ins["consts"] = constants()

    outs = {"y": (P, KT, NT), "kv": (P, 2 * NF, NT), "conv": (P, NC, 2 + 2 * DEC_BATCH), "state": (P, 2, ST, STEP1)}
    nc = bacc.Bacc("TRN2", target_bir_lowering=False, num_devices=1)
    arrays, a, o = {}, {}, {}
    for name, x in ins.items():
        x = np.ascontiguousarray(x)
        arrays[f"in_{name}"] = x
        a[name] = nc.dram_tensor(f"in_{name}", x.shape, mybir.dt.from_np(x.dtype), kind="ExternalInput").ap()
    for name, shape in outs.items():
        o[name] = nc.dram_tensor(f"out_{name}", shape, F32, kind="ExternalOutput").ap()
    build(nc, a, o)
    got = run_bass_kernel_spmd(nc, [arrays], core_ids=[0]).results[0]

    def tokens(x):
        return arr(x).transpose(2, 1, 0).reshape(x.shape[2], -1)

    y, kvt = tokens(got["out_y"]), got["out_kv"]
    kvt = np.stack([tokens(kvt[:, :NF]), tokens(kvt[:, NF:])], axis=1).reshape(NT, 2, N_HEADS, HEAD_DIM)
    conv = tokens(got["out_conv"])
    st = arr(got["out_state"]).transpose(1, 3, 2, 0).reshape(2, STEP1, N_GROUPS, SSM_STATE)
    c = np.ascontiguousarray
    return (c(y[:SEQ][None]), c(y[SEQ:].reshape(DEC_BATCH, DEC_SEQ, D_MODEL)),
            c(kvt[:SEQ][None, None]), c(conv[:2][None, None]), c(st[0, 0][None, None]), c(st[1, 0][None, None]),
            c(kvt[SEQ:].reshape(1, DEC_BATCH, DEC_SEQ, 2, N_HEADS, HEAD_DIM)),
            c(conv[2:].reshape(1, DEC_BATCH, 2, CONV_CH)), c(st[0, 1:][None]), c(st[1, 1:][None]))
```

```python
import math
from contextlib import ExitStack

import concourse.bass as bass
import numpy as np
from concourse import mybir

ALU = mybir.AluOpType
ACT = mybir.ActivationFunctionType
AX = mybir.AxisListType
F32 = mybir.dt.float32
F32R = mybir.dt.float32r
I32 = mybir.dt.int32
ds = bass.ds

P = 128
D_MODEL, SEQ, DEC_BATCH, DEC_SEQ, PAST_LEN = 2048, 256, 8, 8, 2048
NT = SEQ + DEC_BATCH * DEC_SEQ
KT = D_MODEL // P
N_HEADS, HEAD_DIM = 16, 64
ATT_WIDTH = N_HEADS * HEAD_DIM
SSM_WIDTH = CONV_CH = 512
SSM_GROUP, SSM_STATE = 16, 64
N_GROUPS = SSM_WIDTH // SSM_GROUP
ST = N_GROUPS * SSM_STATE // P
D_FF = 5632
FT = D_FF // P
IN_COLS = 5120
ZT = IN_COLS // P
EPS = 1e-6
NEG = -1e30
SCALE = HEAD_DIM ** -0.5
PATTERNS = ((128, 1), (512, 4), (2048, 16))

ZH, ZGB, ZGC, ZU, ZQ, ZK, ZV = 0, 4, 8, 12, 16, 24, 32
NF = 8
NC = 4
SL = SEQ + DEC_BATCH * (DEC_SEQ + 1)
STEP1 = DEC_SEQ + 1
CL = (SEQ + 2) + DEC_BATCH * (DEC_SEQ + 2)

START = 1
ONE_AHEAD = """ps_masked ppt_moved po_moved x_rot y_acc o_scaled o_moved
o_done po_done c_done pt_done ppt_done ssm_h""".split()

KEYS_OLD = 768
KEY_TILES = (KEYS_OLD + 512) // P
NKEYS = KEY_TILES * P + DEC_BATCH * DEC_SEQ
KU = 2 * P
KN = KEY_TILES * P // KU
V_AHEAD = 1
TB = 16

UNIT = 1024
RAW, SPL = 4, 2
U_IN, U_DOWN = D_MODEL // 256, D_FF // 256
N_IN = IN_COLS // 512 * U_IN
N_OUT = D_MODEL // 512 * U_IN
N_GU = 2 * D_FF // 512 * U_IN
N_DN = D_MODEL // 512 * U_DOWN


def multiplicity(dist):
    return sum(((dist >= 0) & (dist <= w) & (dist % d == 0)).astype(np.int64) for w, d in PATTERNS)


def log_mask(count):
    return np.where(count > 0, np.log(np.maximum(count, 1)) / SCALE, NEG).astype(np.float32)


def cache_positions():
    old = np.arange(PAST_LEN - 512)
    return np.concatenate([old[old % 16 < 8], np.arange(PAST_LEN - 512, PAST_LEN)])


def constants():
    t = np.arange(P) % DEC_SEQ
    past = log_mask(multiplicity(PAST_LEN + t[:, None] - cache_positions()[None, :]))
    new = np.full((P, 2 * DEC_BATCH - 1, DEC_SEQ), NEG, np.float32)
    new[:, DEC_BATCH - 1] = log_mask(multiplicity(t[:, None] - np.arange(DEC_SEQ)[None, :]))
    q = np.arange(P)[:, None]
    first = log_mask(multiplicity(q - np.arange(P)[None, :]))
    second = log_mask(multiplicity(q + P - np.arange(2 * P)[None, :]))
    keep = np.ones((P, SL), np.float32)
    keep[:, 0] = 0
    keep[:, SEQ::STEP1] = 0
    return np.concatenate([np.eye(P, dtype=np.float32), past, new.reshape(P, -1), first, second, keep], axis=1)


C_ID, C_PAST = 0, P
C_NEW = C_PAST + KEY_TILES * P
C_PROMPT = C_NEW + (2 * DEC_BATCH - 1) * DEC_SEQ
C_KEEP = C_PROMPT + 3 * P
C_END = C_KEEP + SL

V_MIX, V_OUT, V_FFN, V_FIN, V_D, V_GLU, V_CW = 0, 16, 32, 48, 64, 68, 72
V_ARE, V_AIM, V_DT = 84, 100, 116
V_END = 132


class Steps:

    def __init__(self, eng, sem):
        self.eng, self.sem, self.done, self.it, self.per = eng, sem, 0, None, 0

    def value(self):
        return self.done if self.it is None else self.it * self.per + self.done

    def __call__(self, ins, wait=True):
        ins.then_inc(self.sem, 1)
        self.done += 1
        if wait:
            self.eng.wait_ge(self.sem, self.value())

    def enter(self, it, per):
        self.it, self.per, self.start = it, per, self.done

    def leave(self, n):
        assert self.done - self.start == self.per, (self.done - self.start, self.per)
        self.done = self.start + n * self.per
        self.it = None


def build(nc, a, o):
    with ExitStack() as ctx:
        base = (nc.sbuf_base + 63) // 64 * 64
        top = [base]

        def at(name, shape, dt=F32, offset=None):
            return nc.alloc_sbuf_tensor_at(name, shape, dt, offset=base + offset)

        class Region:

            def __init__(self, start, end):
                self.pos, self.end = start, end

            def take(self, name, shape, dt=F32):
                t = at(name, shape, dt, self.pos)
                self.pos += (4 * int(np.prod(shape[1:])) + 31) // 32 * 32
                assert self.pos <= self.end, (name, self.pos, self.end)
                return t

        X0, XN0 = 5952, 5952 + 20480
        RING0 = XN0 + 40960
        H0 = RING0 + 32768
        END = H0 + 112640
        ZEND = H0 + ZT * NT * 4
        assert base + END <= nc.sbuf_usable_end

        keep = Region(0, X0)
        ident = keep.take("ident", [P, P])
        ones = keep.take("ones", [P, P])
        vec = keep.take("vec", [P, V_END])
        ptmp = at("ptmp", [P, 2, SEQ], F32, keep.pos)
        rstd = keep.take("rstd", [P, NT])
        rtmp = keep.take("rtmp", [P, NT])
        var = keep.take("var", [P, NT])
        halo = keep.take("halo", [P, NC, 2 * DEC_BATCH])

        x1 = at("x1", [P, KT, NT], F32, X0)
        xh = at("xh", [P, KT, NT], F32R, XN0)
        xl = at("xl", [P, KT, NT], F32R, XN0 + KT * NT * 4)
        yout = at("yout", [P, KT, NT], F32, XN0)
        ring = Region(RING0, H0)
        raw = ring.take("raw", [P, RAW, UNIT])
        whi = ring.take("whi", [P, SPL, UNIT], F32R)
        wlo = ring.take("wlo", [P, SPL, UNIT], F32R)
        hh = at("hh", [P, FT, NT], F32R, H0)
        hl = at("hl", [P, FT, NT], F32R, H0 + FT * NT * 4)
        hm = at("hm", [P, FT, NT], F32, H0 + FT * NT * 4)
        z = at("z", [P, ZT, NT], F32, H0)
        upper = Region(ZEND, END)
        vt = upper.take("vt", [P, KEY_TILES, ATT_WIDTH])
        kt = upper.take("kt", [P, 2, NF, KU])
        bt = upper.take("bt", [P, 2, NC, P])
        sq = at("sq", [P, KT, NT], F32, H0 + (FT + KT) * NT * 4)
        sq_last = at("sq_last", [P, KT, NT], F32, XN0 + KT * NT * 4)
        hu = at("hu", [P, FT, NT], F32, H0)
        gate_end = Region(H0 + (FT + 2 * KT) * NT * 4, END)
        rstd3 = at("rstd3", [P, NT], F32, XN0)
        wglu = gate_end.take("wglu", [P, NC, SSM_WIDTH])
        ysig = gate_end.take("ysig", [P, NC, NT])
        deadv = Region(H0 + ZV * NT * 4, ZEND)
        ptk = deadv.take("ptk", [P, KEY_TILES + 1, P])
        deadg = Region(H0 + ZGB * NT * 4, H0 + ZU * NT * 4)
        sp = deadg.take("sp", [P, 2, 3 * P])
        qs = deadg.take("qs", [P, SEQ])
        ks = deadg.take("ks", [P, SEQ])
        vs = deadg.take("vs", [P, 2, P])
        low = Region(XN0, H0)
        const = low.take("const", [P, C_END - P])
        sall = low.take("sall", [P, NKEYS])
        qst = low.take("qst", [P, 2, NF, 32])
        osb = low.take("osb", [P, 2 * P])
        base1 = low.take("base1", [P, 2, ST, TB])
        base16 = low.take("base16", [P, 2, ST, TB + 1])
        vp = low.take("vp", [P, 2, ATT_WIDTH])
        vn = low.take("vn", [P, ATT_WIDTH])
        cmat = low.take("cmat", [P, 2, ST, 32])
        h0 = low.take("h0", [P, 2, ST, DEC_BATCH])
        ho = low.take("ho", [P, 2, ST, STEP1])
        decay = low.take("decay", [P, ST])
        smax = low.take("smax", [P, 6])
        pmax = low.take("pmax", [P, 4, 4])
        us = low.take("us", [P, SL])
        bs = low.take("bs", [P, 2, P])
        cs = low.take("cs", [P, 2, 4, 32])
        ptp = low.take("ptp", [P, 2, 3 * P])
        dcol = low.take("dcol", [P, 1])
        magc = low.take("magc", [P, 2])
        tabc = low.take("tabc", [P, 2, SL])
        tabs = low.take("tabs", [P, 2, SL])
        dec = low.take("dec", [P, 2, SL])
        xr = low.take("xr", [P, 2, SL])
        gr = low.take("gr", [P, 2, SL])
        tm = low.take("tm", [P, 4, SL])
        hb = low.take("hb", [P, 2, 2, SL])
        early = Region(ZEND, H0 + (FT + KT) * NT * 4)
        cu = early.take("cu", [P, NC, CL])
        bmat = early.take("bmat", [P, 2, ST, 32])
        par = early.take("par", [P, 15 + 1, ST])
        pari = early.take("pari", [P, ST], I32)
        base1_made = early.take("base1_made", [P, 2, ST, TB])
        base16_made = early.take("base16_made", [P, 2, ST, TB + 1])
        tmp_place = early.pos
        btmp = early.take("btmp", [P, 4, ST, 32])
        ca = at("ca", [P, NC, CL], F32, tmp_place)
        ctmp = at("ctmp", [P, CL], F32, tmp_place + NC * CL * 4)
        ptmp_made = at("ptmp_made", [P, 2, SEQ], F32, tmp_place)

        ps = ctx.enter_context(nc.psum_tensor("ps", [P, 8, 512], F32))

        names = """b_in den_ready den_turned early_moved const_in vec_in ssm_in glu_in state_stored kv_stored conv_stored stored
        ones_set sq_ready sq_used var_ready root_ready rstd_step rstd_ready m_ready m_hi m_lo
        w_hi w_lo unit_done free0 free1 h_gate h_ready h_hi h_lo y_ready y_step
        vpt_done vp_moved conv_done bt_ready c_ready bt_done bt_moved
        sin_ready sin_done q_zero q_ready pool_step dve_step
        k_used v_used s_masked s_max p_exp pt_done pt_moved o_done o_scaled o_turned o_moved
        q_static ps_done ps_masked ps_max pp_exp pp_norm ppt_done ppt_moved po_done po_moved
        ssm_static tab_ready x_proj x_rot ssm_h c_done y_acc y_glu glu_done glu_sig mixed_done""".split()
        names += [f"x_in{i}" for i in range(4)]
        names += [f"raw_in{i}" for i in range(RAW)] + [f"k_in{i}" for i in range(2)]
        names += [f"v_in{i}" for i in range(KEY_TILES)]
        S = {n: ctx.enter_context(nc.semaphore(n)) for n in names}
        RAW_IN = [S[f"raw_in{i}"] for i in range(RAW)]
        K_IN = [S[f"k_in{i}"] for i in range(2)]
        V_IN = [S[f"v_in{i}"] for i in range(KEY_TILES)]
        FREE = [S["free0"], S["free1"]]

        GEMMS = {"in": (a["w_in"], 0, IN_COLS // 1024, U_IN, 0),
                 "out": (a["w_out"], N_IN, 2, U_IN, 5),
                 "gu": (a["w_gu"], N_IN + N_OUT, D_FF // 512, U_IN, 7),
                 "dn": (a["w_dn"], N_IN + N_OUT + N_GU, 2, U_DOWN, 18)}
        PAIRS = 20

        NORMS = [(0, KT, V_MIX), (0, 4, V_OUT), (4, 8, V_OUT + 4), (12, 4, V_OUT + 12), (0, KT, V_FFN), (0, KT, V_FIN)]
        S3 = 2
        SUM_BANK = (7, 7, 6, 5, 7, 0)

        def tiles_before(k):
            return sum(n for _, n, _ in NORMS[:k])

        def norm_source(k, i, n=1):
            if k in (0, 4, 5):
                return x1[:, i:i + n, :]
            first = {1: ZH, 2: ZQ, 3: ZU}[k]
            return z[:, first + i:first + i + n, :]

        score_turn = {}
        for r in range(2):
            for key in [("s", r, g) for g in range(3)] + [("p", r, e) for e in range(2)]:
                score_turn[key] = len(score_turn)
        turn = {}
        for r in range(2):
            for key in [("pt", r, g) for g in range(3)] + [("pp", r, e) for e in range(2)] + [("o", r, 0)]:
                turn[key] = len(turn)

        def score_bank(*key):
            return score_turn[key] % 2

        def turn_bank(*key):
            return 2 + turn[key] % 2

        block = ctx.enter_context(nc.Block())

        @block.sync
        def _(sy):
            def weights(which):
                src, first, pairs, units, _ = GEMMS[which]
                with sy.Fori(0, pairs) as it:
                    for j in range(2 * units):
                        sy.wait_ge(S["w_lo"], it * (2 * units) + (first + j + 1))
                        sy.dma_start(raw[:, j % RAW, :], src[ds(it * (2 * units) + j, 1), :, :].rearrange("a p n -> p (a n)")) \
                            .then_inc(RAW_IN[j % RAW], 16)

            sy.dma_start(vec[:], a["vecs"]).then_inc(S["vec_in"], 16)
            for c in range(4):
                sy.dma_start(x1[:, 4 * c:4 * c + 4, :], a["xt"][:, 4 * c:4 * c + 4, :]).then_inc(S[f"x_in{c}"], 16)
            sy.dma_start(ident[:], a["consts"][:, 0:P]).then_inc(S["const_in"], 16)
            sy.dma_start(halo[:], a["halo"]).then_inc(S["const_in"], 16)
            sy.dma_start(bmat[:], a["ssm_b"]).then_inc(S["b_in"], 16)
            weights("in")

            def load_k(n, j):
                sy.wait_ge(S["k_used"], n + (j + 1))
                sy.dma_start(kt[:, j % 2], a["ck"][ds(n + j, 1), :, :].rearrange("a p (f k) -> p (a f) k", f=NF)).then_inc(K_IN[j % 2], 16)

            def load_v(n, j):
                sy.wait_ge(S["v_used"], n + (j + 1))
                slot = j % KEY_TILES
                sy.dma_start(vt[:, slot, :], a["cv"][ds(n + j, 1), :, :].rearrange("a p n -> p (a n)")).then_inc(V_IN[slot], 16)

            sy.wait_ge(S["sq_used"], KT)
            for j in range(2):
                load_k(0, j)
            sy.wait_ge(S["conv_done"], 1)
            sy.dma_start(o["conv"][:, :, 0:2], cu[:, :, SEQ:SEQ + 2]).then_inc(S["conv_stored"], 16)
            for c in range(NC):
                sy.dma_start(o["conv"][:, c, 2:18].rearrange("p (b j) -> p b j", j=2),
                             cu[:, c, SEQ + 2:CL].rearrange("p (b s) -> p b s", s=DEC_SEQ + 2)[:, :, DEC_SEQ:]) \
                    .then_inc(S["conv_stored"], 16)
            for g in range(2):
                sy.wait_ge(FREE[g], 1 + ZV // 8)
            sy.dma_start(o["kv"][:, 0:NF, :], z[:, ZK:ZV, :]).then_inc(S["kv_stored"], 16)
            sy.wait_ge(S["unit_done"], SPL + N_IN)
            sy.dma_start(const[:], a["consts"][:, P:C_END]).then_inc(S["const_in"], 16)
            for g in range(2):
                sy.wait_ge(FREE[g], 1 + IN_COLS // 1024)
            sy.dma_start(o["kv"][:, NF:2 * NF, :], z[:, ZV:ZT, :]).then_inc(S["kv_stored"], 16)
            sy.dma_start(cmat[:], a["ssm_c"]).then_inc(S["ssm_in"], 16)
            sy.dma_start(h0[:], a["state"]).then_inc(S["ssm_in"], 16)
            sy.wait_ge(S["conv_stored"], 16 * (1 + NC))
            sy.wait_ge(S["early_moved"], 3)
            sy.wait_ge(S["bt_done"], 2)

            def rest(it, r):
                for j in range(V_AHEAD):
                    load_v(it * (2 * KEY_TILES), KEY_TILES * r + j)
                for j in range(2, KN):
                    load_k(it * (2 * KN), KN * r + j)
                for j in range(V_AHEAD, KEY_TILES):
                    load_v(it * (2 * KEY_TILES), KEY_TILES * r + j)

            def first_keys(it, r):
                for j in range(2):
                    load_k(it * (2 * KN), KN * r + j)

            rest(0, 0)
            with sy.Fori(0, NC - 1) as it:
                for r in range(1, 3):
                    first_keys(it, r)
                    rest(it, r)
            first_keys(NC - 1, 1)
            rest(NC - 1, 1)
            sy.wait_ge(S["k_used"], 2 + DEC_BATCH * KN)
            sy.dma_start(wglu[:], a["w_glu"]).then_inc(S["glu_in"], 16)
            sy.wait_ge(S["y_acc"], NC + START)
            sy.dma_start(o["state"], ho[:]).then_inc(S["state_stored"], 16)
            sy.wait_ge(S["po_moved"], 2 * NC + START)
            sy.wait_ge(S["o_moved"], 8 * NC + START)
            sy.wait_ge(S["state_stored"], 16)
            weights("out")
            weights("gu")
            weights("dn")
            for c in range(4):
                sy.wait_ge(S["y_ready"], 4 * (c + 1))
                sy.dma_start(o["y"][:, 4 * c:4 * c + 4, :], yout[:, 4 * c:4 * c + 4, :]).then_inc(S["stored"], 16)
            sy.wait_ge(S["kv_stored"], 32)
            sy.wait_ge(S["conv_stored"], 16 * (1 + NC))
            sy.wait_ge(S["glu_in"], 16)
            sy.wait_ge(S["stored"], 64)

        @block.scalar
        def _(act):
            def square(k, c):
                i = NORMS[k][0] + 4 * c
                dst = sq_last if k == 5 else sq
                act.activation(dst[:, i:i + 4, :], norm_source(k, 4 * c, 4), ACT.Square).then_inc(S["sq_ready"], 1)

            def root(k):
                act.wait_ge(S["var_ready"], k + 1)
                act.activation(rtmp[:], var[:], ACT.Sqrt).then_inc(S["root_ready"], 1)

            def high(first, n):
                for i in range(first, first + n):
                    act.wait_ge(S["m_ready"], i + 1)
                    act.activation(hh[:, i, :], hm[:, i, :], ACT.Copy).then_inc(S["m_hi"], 1)

            def gained_high(k, c):
                for i in range(4 * c, 4 * c + 4):
                    gain = NORMS[k][2] + i
                    act.activation(xh[:, i, :], x1[:, i, :], ACT.Copy, scale=vec[:, gain:gain + 1]).then_inc(S["m_hi"], 1)

            def split(which, it, j):
                _, first, _, units, _ = GEMMS[which]
                act.wait_ge(RAW_IN[j % RAW], it * (16 * 2 * units // RAW) + 16 * ((first + j) // RAW + 1))
                act.wait_ge(S["unit_done"], it * (2 * units) + (first + j + 1))
                act.activation(whi[:, j % SPL, :], raw[:, j % RAW, :], ACT.Copy).then_inc(S["w_hi"], 1)

            act.wait_ge(S["vec_in"], 16)
            for c in range(4):
                act.wait_ge(S[f"x_in{c}"], 16)
                gained_high(0, c)
                if c < 3:
                    square(0, c)

            for j in range(2 * U_IN):
                split("in", 0, j)
                if j == 1:
                    square(0, 3)
                if j == U_IN + 1:
                    root(0)
                if j == U_IN + 4:
                    act.wait_ge(S["sin_ready"], 2)
                    act.activation(par[:, 14:16, :], par[:, 12:14, :], ACT.Sin).then_inc(S["sin_done"], 1)
            with act.Fori(1, IN_COLS // 1024) as it:
                for j in range(2 * U_IN):
                    split("in", it, j)

            for c in range(6):
                act.wait_ge(S["vpt_done"], c + 1)
                dst = vp[:, c // 2, 512 * (c % 2):512 * (c % 2) + 512] if c < 4 else vn[0:64, 512 * (c - 4):512 * (c - 3)]
                act.activation(dst, ps[0:(P if c < 4 else 64), c, :], ACT.Copy).then_inc(S["vp_moved"], 1)

            act.wait_ge(S["q_zero"], 1)

            def queries(it, r):
                act.wait_ge(S["k_used"], it * (2 * KN) + (2 if r == 0 else 2 + KN))
                for e in range(2):
                    h = slice(64 * e, 64 * e + 64)
                    for i in range(2):
                        act.activation(qst[h, r, i:NF:2, 16 * i + 8 * e:16 * i + 8 * e + 8],
                                       z[h, ZQ + i:ZQ + NF:2, ds(it * 16 + (SEQ + 8 * r), 8)], ACT.Copy).then_inc(S["q_ready"], 1)

            with act.Fori(0, NC) as it:
                for r in range(2):
                    queries(it, r)
                    act.wait_ge(S["s_max"], it * 2 + (r + 1))
                    act.activation(sall[:], sall[:], ACT.Exp, bias=smax[:, 3:4], scale=SCALE, accum_out=smax[:, 4:5]).then_inc(S["p_exp"], 1)
                    for e in range(2):
                        for t in range(2):
                            act.wait_ge(S["ps_max"], it * 4 + (2 * r + e + 1))
                            lo, hi = (0, P) if t == 0 else (P, 3 * P)
                            act.activation(sp[:, e, lo:hi], sp[:, e, lo:hi], ACT.Exp, bias=pmax[:, 1, 2 * e + t:2 * e + t + 1],
                                           scale=SCALE, accum_out=pmax[:, 2, 2 * e + t:2 * e + t + 1]).then_inc(S["pp_exp"], 1)
                    for g in range(3):
                        act.wait_ge(S["pt_done"], it * 6 + (3 * r + g + 1) + START)
                        if g == 0:
                            act.wait_ge(S["o_done"], it * 2 + r + START)
                        b = turn_bank("pt", r, g)
                        w = 4 if g < 2 else 2
                        act.activation(ptk[:, 4 * g:4 * g + w, :].rearrange("p a n -> p (a n)"), ps[:, b, 0:w * P], ACT.Copy) \
                            .then_inc(S["pt_moved"], 1)
                        if g == 2:
                            act.activation(ptk[0:64, KEY_TILES, :], ps[0:64, b, 256:384], ACT.Copy).then_inc(S["pt_moved"], 1)
                    for e in range(2):
                        act.wait_ge(S["ppt_done"], it * 4 + (2 * r + e + 1) + START)
                        act.wait_ge(S["po_done"], it * 4 + (2 * r) + START)
                        act.activation(ptp[:, e], ps[:, turn_bank("pp", r, e), 0:3 * P], ACT.Copy).then_inc(S["ppt_moved"], 1)
                    act.wait_ge(S["po_done"], it * 4 + (2 * r + 2) + START)
                    act.activation(z[:, ds(it * 2 + (ZQ + r), 1), 0:SEQ].rearrange("p a n -> p (a n)"), ps[:, 4, 0:SEQ], ACT.Copy) \
                        .then_inc(S["po_moved"], 1)

            act.wait_ge(S["o_moved"], 8 * NC + START)
            act.wait_ge(S["po_moved"], 2 * NC + START)
            square(1, 0)
            for c in range(2):
                square(2, c)
            act.wait_ge(S["y_acc"], NC + START)
            for c in range(NC):
                act.activation(z[:, ZU + c, :], z[:, ZU + c, :], ACT.Gelu_apprx_tanh).then_inc(S["y_glu"], 1)
            root(1)
            high(0, 4)
            for c in range(NC):
                act.wait_ge(S["glu_done"], c + 1)
                act.activation(ysig[:, c, :], ps[:, c, 0:NT], ACT.Sigmoid, bias=vec[:, V_GLU + c:V_GLU + c + 1]) \
                    .then_inc(S["glu_sig"], 1)
            for j in range(2):
                split("out", 0, j)
            act.wait_ge(S["mixed_done"], 1)
            square(3, 0)
            root(2)
            for j in range(2, 6):
                high(2 * j, 2)
                split("out", 0, j)
                if j == 3:
                    root(3)
            high(12, 4)

            def new_x(k, it, g):
                act.wait_ge(FREE[g], (7 if k == 4 else PAIRS) - 2 + it + 2)
                if k == 4:
                    gained_high(4, 2 * it + g)
                square(k, 2 * it + g)

            def x_pair(which, k, it, start=0):
                units = GEMMS[which][3]
                for j in range(start, 2 * units):
                    split(which, it, j)
                    if j == 3 and it:
                        new_x(k, 0, 1)
                    if j == units + 3:
                        new_x(k, it, 0)

            x_pair("out", 4, 0, 6)
            x_pair("out", 4, 1)
            new_x(4, 1, 1)

            def silu(it):
                act.wait_ge(FREE[0], it + (1 + 7 + 1))
                act.activation(hm[:, ds(it * 4, 4), :], hm[:, ds(it * 4, 4), :], ACT.Silu).then_inc(S["h_gate"], 1)

            def h_high(it):
                act.wait_ge(S["h_ready"], it + 1)
                act.activation(hh[:, ds(it * 4, 4), :], hm[:, ds(it * 4, 4), :], ACT.Copy).then_inc(S["h_hi"], 1)

            def gu_pair(it, first):
                for j in range(2 * U_IN):
                    split("gu", it, j)
                    if j == 4 and not first:
                        h_high(it - 1)
                    if j == U_IN + 1 and first:
                        root(4)
                    if j == U_IN + 3:
                        silu(it)

            gu_pair(0, True)
            with act.Fori(1, D_FF // 512) as it:
                gu_pair(it, False)
            h_high(D_FF // 512 - 1)
            x_pair("dn", 5, 0)
            x_pair("dn", 5, 1)
            new_x(5, 1, 1)
            root(5)

        @block.vector
        def _(dve):
            v = nc.vector
            dve.sem_inc(S["w_lo"], RAW)
            v.memset(ones[:], 1.0).then_inc(S["ones_set"], 1)
            rstd_step = Steps(dve, S["rstd_step"])

            def scales(k, rstd=rstd):
                dve.wait_ge(S["sq_used"], tiles_before(k + 1))
                v.tensor_scalar(var[:], ps[:, SUM_BANK[k], 0:NT], 1.0 / (P * NORMS[k][1]), EPS, ALU.mult, ALU.add).then_inc(S["var_ready"], 1)
                dve.wait_ge(S["root_ready"], k + 1)
                rstd_step(v.reciprocal(rstd[:], rtmp[:]))
                rstd_step(v.tensor_tensor(rtmp[:], rstd[:], rstd[:], ALU.mult))
                rstd_step(v.tensor_tensor(rtmp[:], rtmp[:], var[:], ALU.mult))
                rstd_step(v.tensor_scalar(rtmp[:], rtmp[:], -0.5, 1.5, ALU.mult, ALU.add))
                v.tensor_tensor(rstd[:], rstd[:], rtmp[:], ALU.mult).then_inc(S["rstd_ready"], 1)
                dve.wait_ge(S["rstd_ready"], k + 1)

            rstd4 = rstd[:].rearrange("p (a n) -> p a n", a=1).to_broadcast([P, 4, NT])

            def norm_low(i):
                dve.wait_ge(S["m_hi"], KT + i + 1)
                v.tensor_tensor(hl[:, i, :], hm[:, i, :], hh[:, i, :].bitcast(F32), ALU.subtract).then_inc(S["m_lo"], 1)

            def norm(k, start=0, n=None):
                first, tiles, gain = NORMS[k]
                n = n or tiles
                if start == 0 and k != 3:
                    scales(k)
                for i in range(start, start + n):
                    dst, done = (yout[:, i, :], S["y_ready"]) if k == 5 else (hm[:, first + i, :], S["m_ready"])
                    v.scalar_tensor_tensor(out=dst, in0=norm_source(k, i)[:, 0, :], scalar=vec[:, gain + i:gain + i + 1],
                                           in1=(rstd3 if k == 3 else rstd)[:], op0=ALU.mult, op1=ALU.mult).then_inc(done, 1)
                    if k < 5 and i > start:
                        norm_low(first + i - 1)
                if k < 5:
                    norm_low(first + start + n - 1)

            def gained_low(k, c):
                for i in range(4 * c, 4 * c + 4):
                    gain = NORMS[k][2] + i
                    dve.wait_ge(S["m_hi"], (0 if k == 0 else 2 * KT) + i + 1)
                    v.scalar_tensor_tensor(out=xl[:, i, :], in0=x1[:, i, :], scalar=vec[:, gain:gain + 1],
                                           in1=xh[:, i, :].bitcast(F32), op0=ALU.mult, op1=ALU.subtract).then_inc(S["m_lo"], 1)

            def split(which, it, j):
                _, first, _, units, _ = GEMMS[which]
                dve.wait_ge(S["w_hi"], it * (2 * units) + (first + j + 1))
                v.tensor_tensor(wlo[:, j % SPL, :], raw[:, j % RAW, :], whi[:, j % SPL, :].bitcast(F32), ALU.subtract) \
                    .then_inc(S["w_lo"], 1)

            dve.wait_ge(S["vec_in"], 16)
            for c in range(4):
                gained_low(0, c)

            def z_out(it, g):
                dve.wait_ge(S["unit_done"], it * (2 * U_IN) + (SPL + U_IN * (g + 1)))
                v.tensor_tensor(z[:, ds(it * 8 + 4 * g, 4), :], ps[:, 4 * g:4 * g + 4, 0:NT], rstd4, ALU.mult).then_inc(FREE[g], 1)

            def z_pair(it, first):
                for j in range(2 * U_IN):
                    split("in", it, j)
                    if j == 1 and not first:
                        z_out(it - 1, 1)
                    if j == U_IN + 1:
                        if first:
                            scales(0)
                        z_out(it, 0)
                    if j == U_IN + 4 and first:
                        dve.wait_ge(S["den_ready"], 1)
                        v.reciprocal(par[:, 4, :], par[:, 3, :]).then_inc(S["den_turned"], 1)

            z_pair(0, True)
            with dve.Fori(1, IN_COLS // 1024) as it:
                z_pair(it, False)
            z_out(IN_COLS // 1024 - 1, 1)

            dve.wait_ge(S["ssm_in"], 32)
            v.tensor_scalar(cmat[:, 1], cmat[:, 1], -1.0, None, ALU.mult).then_inc(S["c_ready"], 1)
            dve.wait_ge(S["bt_done"], 2)
            for i in range(2):
                v.tensor_copy(bt[:, i].rearrange("p c n -> p (c n)"), ps[:, 6 + i, :]).then_inc(S["bt_moved"], 1)
            dve.wait_ge(S["const_in"], 48)
            dve.wait_ge(S["conv_done"], 1)

            with dve.Fori(0, NC) as it:
                step = Steps(dve, S["dve_step"])
                step.enter(it, 79)

                def scan(i):
                    b = i % 2
                    c_, s_ = tabc[:, b, :], tabs[:, b, :]
                    dve.wait_ge(S["tab_ready"], it * 4 + (i + 1))
                    dve.wait_ge(S["x_proj"], it * 4 + (i + 1))
                    xre, xim = ps[:, 6, 0:SL], ps[:, 7, 0:SL]
                    step(v.tensor_tensor(tm[:, 0], xre, c_, ALU.mult), wait=False)
                    step(v.tensor_tensor(tm[:, 1], xim, s_, ALU.mult), wait=False)
                    step(v.tensor_tensor(tm[:, 2], xim, c_, ALU.mult))
                    v.tensor_tensor(tm[:, 3], xre, s_, ALU.mult).then_inc(S["x_rot"], 1)
                    step(v.tensor_tensor(xr[:, 0], tm[:, 0], tm[:, 1], ALU.add))
                    dve.wait_ge(S["x_rot"], it * 4 + (i + 1) + START)
                    step(v.tensor_tensor(xr[:, 1], tm[:, 2], tm[:, 3], ALU.subtract))
                    step(v.tensor_copy(xr[:, :, SEQ:SL:STEP1].rearrange("p a (c b) -> p a c b", c=1),
                                       h0[:, :, ds(it * 4 + i, 1), :]))
                    for a_ in range(2):
                        step(v.tensor_tensor_scan(gr[:, a_, :], dec[:, b, :], xr[:, a_, :], 0.0, ALU.mult, ALU.add), wait=a_ == 1)
                    step(v.tensor_tensor(tm[:, 0], gr[:, 0], c_, ALU.mult), wait=False)
                    step(v.tensor_tensor(tm[:, 1], gr[:, 1], s_, ALU.mult), wait=False)
                    step(v.tensor_tensor(tm[:, 2], gr[:, 0], s_, ALU.mult), wait=False)
                    step(v.tensor_tensor(tm[:, 3], gr[:, 1], c_, ALU.mult))
                    dve.wait_ge(S["c_done"], it * 4 + max(i - 1, 0) + START)
                    step(v.tensor_tensor(hb[:, b, 0], tm[:, 0], tm[:, 1], ALU.subtract))
                    v.tensor_tensor(hb[:, b, 1], tm[:, 2], tm[:, 3], ALU.add).then_inc(S["ssm_h"], 1)
                    dve.wait_ge(S["ssm_h"], it * 4 + (i + 1) + START)
                    step(v.tensor_copy(ho[:, :, ds(it * 4 + i, 1), :],
                                       hb[:, b, :, SEQ - 1:SL:STEP1].rearrange("p a (c k) -> p a c k", c=1)))

                for r in range(2):
                    dve.wait_ge(S["pt_done"], it * 6 + 3 * r + START)
                    for g in range(3):
                        dve.wait_ge(S["k_used"], it * (2 * KN) + (2 + KN * r + min(2 * (g + 1), KN)))
                        b = score_bank("s", r, g)
                        w = 512 if g < 2 else 256
                        c0 = C_PAST - P + 512 * g
                        v.tensor_tensor(sall[:, 512 * g:512 * g + w], ps[:, b, 0:w], const[:, c0:c0 + w], ALU.add) \
                            .then_inc(S["s_masked"], 1)
                        if g == 1:
                            dve.wait_ge(S["s_masked"], it * 8 + (4 * r + 2))
                            step(v.tensor_reduce(smax[:, 0:1], sall[:, 0:1024], AX.X, ALU.max), wait=False)
                    new = C_NEW - P + 8 * (DEC_BATCH - 1 - r)
                    v.tensor_tensor(sall[:, KEY_TILES * P:NKEYS], ps[:, b, 256:320], const[:, ds(it * -16 + new, 64)], ALU.add) \
                        .then_inc(S["s_masked"], 1)
                    dve.wait_ge(S["s_masked"], it * 8 + (4 * r + 4))
                    step(v.tensor_reduce(smax[:, 1:2], sall[:, 1024:NKEYS], AX.X, ALU.max))
                    step(v.tensor_tensor(smax[:, 2:3], smax[:, 0:1], smax[:, 1:2], ALU.max))
                    v.tensor_scalar(smax[:, 3:4], smax[:, 2:3], -SCALE, None, ALU.mult).then_inc(S["s_max"], 1)
                    for e in range(2):
                        dve.wait_ge(S["ps_done"], it * 4 + (2 * r + e + 1))
                        if e == 0:
                            dve.wait_ge(S["ppt_done"], it * 4 + 2 * r + START)
                        v.tensor_tensor(sp[:, e], ps[:, score_bank("p", r, e), 0:3 * P], const[:, C_PROMPT - P:C_PROMPT + 2 * P], ALU.add) \
                            .then_inc(S["ps_masked"], 1)
                        dve.wait_ge(S["ps_masked"], it * 4 + (2 * r + e + 1) + START)
                        step(v.tensor_reduce(pmax[:, 0, 2 * e:2 * e + 1], sp[:, e, 0:P], AX.X, ALU.max), wait=False)
                        step(v.tensor_reduce(pmax[:, 0, 2 * e + 1:2 * e + 2], sp[:, e, P:3 * P], AX.X, ALU.max))
                        v.tensor_scalar(pmax[:, 1, 2 * e:2 * e + 2], pmax[:, 0, 2 * e:2 * e + 2], -SCALE, None, ALU.mult) \
                            .then_inc(S["ps_max"], 1)
                    dve.wait_ge(S["pp_exp"], it * 8 + (4 * r + 4))
                    step(v.reciprocal(pmax[:, 3, :], pmax[:, 2, :]))
                    for e in range(2):
                        step(v.tensor_scalar(sp[:, e, 0:P], sp[:, e, 0:P], pmax[:, 3, 2 * e:2 * e + 1], None, ALU.mult), wait=False)
                        v.tensor_scalar(sp[:, e, P:3 * P], sp[:, e, P:3 * P], pmax[:, 3, 2 * e + 1:2 * e + 2], None, ALU.mult) \
                            .then_inc(S["pp_norm"], 1)
                    scan(2 * r)
                    dve.wait_ge(S["p_exp"], it * 2 + (r + 1))
                    step(v.reciprocal(smax[:, 5:6], smax[:, 4:5]))
                    dve.wait_ge(S["o_done"], it * 2 + (r + 1) + START)
                    v.tensor_scalar(osb[:], ps[:, 4, 0:2 * P], smax[:, 5:6], None, ALU.mult).then_inc(S["o_scaled"], 1)
                    dve.wait_ge(S["o_turned"], it * 2 + (r + 1))
                    for e in range(2):
                        for i in range(2):
                            src = ps[64 * e:64 * e + 64, turn_bank("o", r, 0), P * i:P * i + P].rearrange("p (c n) -> p c n", n=32)
                            v.tensor_copy(z[64 * e:64 * e + 64, ZQ + i:ZQ + NF:2, ds(it * 16 + (SEQ + 8 * r), 8)],
                                          src[:, :, 16 * i + 8 * e:16 * i + 8 * e + 8]).then_inc(S["o_moved"], 1)
                    scan(2 * r + 1)
                dve.wait_ge(S["c_done"], it * 4 + 4 + START)
                yb = z[:, ds(it + ZU, 1), :].rearrange("p a n -> p (a n)")
                step(v.scalar_tensor_tensor(out=yb[:, 0:SEQ], in0=us[:, 0:SEQ], scalar=dcol[:], in1=ps[:, 5, 0:SEQ],
                                            op0=ALU.mult, op1=ALU.add), wait=False)
                tail = lambda x: x.rearrange("p (b s) -> p b s", s=STEP1)[:, :, 1:]
                v.scalar_tensor_tensor(out=yb[:, SEQ:NT].rearrange("p (b s) -> p b s", s=DEC_SEQ), in0=tail(us[:, SEQ:SL]),
                                       scalar=dcol[:], in1=tail(ps[:, 5, SEQ:SL]), op0=ALU.mult, op1=ALU.add).then_inc(S["y_acc"], 1)
                step.leave(NC)

            norm(1)
            for j in range(2):
                split("out", 0, j)
            for c in range(NC):
                dve.wait_ge(S["glu_sig"], c + 1)
                if c == 0:
                    dve.wait_ge(S["glu_done"], NC)
                v.tensor_tensor(z[:, ZU + c, :], z[:, ZU + c, :], ysig[:, c, :], ALU.mult) \
                    .then_inc(S["y_step"] if c < NC - 1 else S["mixed_done"], 1)
            dve.wait_ge(S["y_step"], NC - 1)
            for j in range(2, 6):
                norm(2, 2 * j - 4, 2)
                split("out", 0, j)
                if j == 3:
                    scales(3, rstd3)
            norm(3)

            def x_out(which, it, g):
                _, first, _, units, _ = GEMMS[which]
                dve.wait_ge(S["unit_done"], it * (2 * units) + (SPL + first + units * (g + 1)))
                t = x1[:, ds(it * 8 + 4 * g, 4), :]
                v.tensor_tensor(t, ps[:, 4 * g:4 * g + 4, 0:NT], t, ALU.add).then_inc(FREE[g], 1)

            def x_pair(which, it, start=0):
                units = GEMMS[which][3]
                for j in range(start, 2 * units):
                    split(which, it, j)
                    if j == 1 and it:
                        x_out(which, it - 1, 1)
                    if j == 5 and it and which == "out":
                        gained_low(4, 2 * it - 1)
                    if j == units + 1:
                        x_out(which, it, 0)
                    if j == units + 5 and which == "out":
                        gained_low(4, 2 * it)

            x_pair("out", 0, 6)
            x_pair("out", 1)
            x_out("out", 1, 1)
            gained_low(4, 3)

            def gate_scaled(it):
                dve.wait_ge(S["unit_done"], it * (2 * U_IN) + (SPL + N_IN + N_OUT + U_IN))
                v.tensor_tensor(hm[:, ds(it * 4, 4), :], ps[:, 0:4, 0:NT], rstd4, ALU.mult).then_inc(FREE[0], 1)

            def up_scaled(it):
                dve.wait_ge(S["unit_done"], it * (2 * U_IN) + (SPL + N_IN + N_OUT + 2 * U_IN))
                v.tensor_tensor(hu[:, ds(it * 4, 4), :], ps[:, 4:8, 0:NT], rstd4, ALU.mult).then_inc(FREE[1], 1)

            def gate(it):
                dve.wait_ge(S["h_gate"], it + 1)
                dve.wait_ge(FREE[1], it + (1 + 7 + 1))
                t = hm[:, ds(it * 4, 4), :]
                v.tensor_tensor(t, hu[:, ds(it * 4, 4), :], t, ALU.mult).then_inc(S["h_ready"], 1)

            def h_low(it):
                dve.wait_ge(S["h_hi"], it + 1)
                v.tensor_tensor(hl[:, ds(it * 4, 4), :], hm[:, ds(it * 4, 4), :], hh[:, ds(it * 4, 4), :].bitcast(F32), ALU.subtract) \
                    .then_inc(S["h_lo"], 1)

            def gu_pair(it, first):
                for j in range(2 * U_IN):
                    split("gu", it, j)
                    if j == 1 and not first:
                        up_scaled(it - 1)
                    if j == 2 and not first:
                        gate(it - 1)
                    if j == 6 and not first:
                        h_low(it - 1)
                    if j == U_IN + 1:
                        if first:
                            scales(4)
                        gate_scaled(it)

            gu_pair(0, True)
            with dve.Fori(1, D_FF // 512) as it:
                gu_pair(it, False)
            up_scaled(D_FF // 512 - 1)
            gate(D_FF // 512 - 1)
            h_low(D_FF // 512 - 1)
            x_pair("dn", 0)
            x_pair("dn", 1)
            x_out("dn", 1, 1)
            norm(5)

        @block.gpsimd
        def _(pool):
            g_ = nc.gpsimd
            step = Steps(pool, S["pool_step"])
            are, aim, ldt = (vec[:, c:c + ST] for c in (V_ARE, V_AIM, V_DT))

            def arr(i):
                return par[:, i, :]

            def both(out, x, scalar, y, first, second, tmp=None):
                tmp = arr(11) if tmp is None else tmp
                step(g_.tensor_scalar(tmp, x, scalar, None, first))
                step(g_.tensor_tensor(out, tmp, y, second))

            def round_to(out, x, scale):
                step(g_.tensor_scalar(out, x, scale, 12582912.0, ALU.mult, ALU.add))
                step(g_.tensor_scalar(out, out, -12582912.0, None, ALU.add))

            def exp(out, x, k, r):
                step(g_.tensor_scalar(r, x, 88.0, -87.0, ALU.min, ALU.max))
                round_to(k, r, math.log2(math.e))
                both(r, k, -0.693359375, r, ALU.mult, ALU.add)
                both(r, k, 2.12194440e-4, r, ALU.mult, ALU.add)
                step(g_.tensor_scalar(out, r, 1.0 / math.factorial(8), None, ALU.mult))
                for n in range(7, 0, -1):
                    both(out, out, 1.0 / math.factorial(n), r, ALU.add, ALU.mult)
                step(g_.tensor_scalar(out, out, 1.0, None, ALU.add))
                step(g_.tensor_scalar(k, k, 127.0, 1.0, ALU.add, ALU.max))
                step(g_.tensor_scalar(k, k, 8388608.0, None, ALU.mult))
                step(g_.tensor_copy(pari[:], k))
                step(g_.tensor_tensor(out, out, pari[:].bitcast(F32), ALU.mult))

            pool.wait_ge(S["vec_in"], 16)
            DT, MAG, ANG = 0, 1, 2
            exp(arr(DT), ldt, arr(3), arr(4))
            step(g_.tensor_tensor(arr(5), are, arr(DT), ALU.mult))
            exp(arr(MAG), arr(5), arr(3), arr(4))
            step(g_.tensor_tensor(arr(ANG), aim, arr(DT), ALU.mult))
            round_to(arr(3), arr(ANG), 1.0 / (2 * math.pi))
            turns = [6.28125, 0.0019350051879882812, 3.019916050e-07]
            both(arr(4), arr(3), -turns[0], arr(ANG), ALU.mult, ALU.add)
            for part in turns[1:]:
                both(arr(4), arr(3), -part, arr(4), ALU.mult, ALU.add)
            g_.tensor_scalar(arr(12), arr(4), 3.1415925, -3.1415925, ALU.min, ALU.max).then_inc(S["sin_ready"], 1)
            pool.wait_ge(S["sin_ready"], 1)
            step(g_.tensor_tensor(arr(3), are, are, ALU.mult))
            step(g_.tensor_tensor(arr(4), aim, aim, ALU.mult))
            g_.tensor_tensor(arr(3), arr(3), arr(4), ALU.add).then_inc(S["den_ready"], 1)
            g_.tensor_scalar(arr(13), arr(12), 0.5, None, ALU.mult).then_inc(S["sin_ready"], 1)
            pool.wait_ge(S["sin_done"], 1)
            SIN, COS = 14, 15
            step(g_.tensor_tensor(arr(COS), arr(COS), arr(COS), ALU.mult))
            step(g_.tensor_scalar(arr(COS), arr(COS), -2.0, 1.0, ALU.mult, ALU.add))
            step(g_.tensor_tensor(arr(5), arr(COS), arr(COS), ALU.mult))
            step(g_.tensor_tensor(arr(6), arr(SIN), arr(SIN), ALU.mult))
            step(g_.tensor_tensor(arr(5), arr(5), arr(6), ALU.add))
            step(g_.tensor_scalar(arr(5), arr(5), -0.5, 1.5, ALU.mult, ALU.add))
            step(g_.tensor_tensor(arr(COS), arr(COS), arr(5), ALU.mult))
            step(g_.tensor_tensor(arr(SIN), arr(SIN), arr(5), ALU.mult))
            step(g_.tensor_tensor(arr(7), arr(MAG), arr(COS), ALU.mult))
            step(g_.tensor_scalar(arr(7), arr(7), -1.0, None, ALU.add))
            step(g_.tensor_tensor(arr(8), arr(MAG), arr(SIN), ALU.mult))
            pool.wait_ge(S["den_turned"], 1)
            step(g_.tensor_tensor(arr(5), arr(7), are, ALU.mult))
            step(g_.tensor_tensor(arr(6), arr(8), aim, ALU.mult))
            step(g_.tensor_tensor(arr(5), arr(5), arr(6), ALU.add))
            step(g_.tensor_tensor(arr(9), arr(5), arr(4), ALU.mult))
            step(g_.tensor_tensor(arr(5), arr(8), are, ALU.mult))
            step(g_.tensor_tensor(arr(6), arr(7), aim, ALU.mult))
            step(g_.tensor_tensor(arr(5), arr(5), arr(6), ALU.subtract))
            step(g_.tensor_tensor(arr(10), arr(5), arr(4), ALU.mult))
            pool.wait_ge(S["b_in"], 16)

            def cf(i):
                return par[:, i, :].rearrange("p (s a) -> p s a", a=1).to_broadcast([P, ST, 32])

            step(g_.tensor_tensor(btmp[:, 0], bmat[:, 0], cf(9), ALU.mult))
            step(g_.tensor_tensor(btmp[:, 1], bmat[:, 1], cf(10), ALU.mult))
            step(g_.tensor_tensor(btmp[:, 2], bmat[:, 1], cf(9), ALU.mult))
            step(g_.tensor_tensor(btmp[:, 3], bmat[:, 0], cf(10), ALU.mult))
            g_.tensor_tensor(bmat[:, 0], btmp[:, 0], btmp[:, 1], ALU.subtract).then_inc(S["bt_ready"], 1)
            g_.tensor_tensor(bmat[:, 1], btmp[:, 2], btmp[:, 3], ALU.add).then_inc(S["bt_ready"], 1)

            def powers(c_, s_):
                k = 1
                while k < TB:
                    ck_, sk_ = (x[:, :, k - 1:k].to_broadcast([P, ST, k]) for x in (c_, s_))
                    q = [ptmp_made[:, j // 2, P * (j % 2):P * (j % 2) + ST * k].rearrange("p (s n) -> p s n", n=k) for j in range(4)]
                    step(g_.tensor_tensor(q[0], c_[:, :, 0:k], ck_, ALU.mult), wait=False)
                    step(g_.tensor_tensor(q[1], s_[:, :, 0:k], sk_, ALU.mult), wait=False)
                    step(g_.tensor_tensor(q[2], c_[:, :, 0:k], sk_, ALU.mult), wait=False)
                    step(g_.tensor_tensor(q[3], s_[:, :, 0:k], ck_, ALU.mult))
                    step(g_.tensor_tensor(c_[:, :, k:2 * k], q[0], q[1], ALU.subtract), wait=False)
                    step(g_.tensor_tensor(s_[:, :, k:2 * k], q[2], q[3], ALU.add))
                    k *= 2
                q0, q1 = (ptmp_made[:, j, :].rearrange("p (s n) -> p s n", n=TB) for j in range(2))
                step(g_.tensor_tensor(q0, c_, c_, ALU.mult), wait=False)
                step(g_.tensor_tensor(q1, s_, s_, ALU.mult))
                step(g_.tensor_tensor(q0, q0, q1, ALU.add))
                step(g_.tensor_scalar(q0, q0, -0.5, 1.5, ALU.mult, ALU.add))
                step(g_.tensor_tensor(c_, c_, q0, ALU.mult), wait=False)
                step(g_.tensor_tensor(s_, s_, q0, ALU.mult))

            for j in range(2):
                step(g_.tensor_copy(base1_made[:, j, :, 0:1], par[:, 15 - j, :].rearrange("p (s n) -> p s n", n=1)))
            powers(base1_made[:, 0], base1_made[:, 1])
            step(g_.tensor_copy(base16_made[:, :, :, 1:2], base1_made[:, :, :, TB - 1:TB]), wait=False)
            for j, one in ((0, 1.0), (1, 0.0)):
                step(g_.memset(base16_made[:, j, :, 0:1], one))
            powers(base16_made[:, 0, :, 1:], base16_made[:, 1, :, 1:])

            for g in range(2):
                pool.wait_ge(FREE[g], 1 + 2)
            pool.wait_ge(S["const_in"], 32)
            sam = cu[:, :, SEQ + 2:CL].rearrange("p c (b s) -> p c b s", s=DEC_SEQ + 2)
            zs = lambda t: z[:, t:t + NC, SEQ:NT].rearrange("p c (b s) -> p c b s", s=DEC_SEQ)
            step(g_.memset(cu[:, :, 0:2], 0.0), wait=False)
            step(g_.tensor_tensor(cu[:, :, 2:SEQ + 2], z[:, ZGC:ZGC + NC, 0:SEQ], z[:, ZH:ZH + NC, 0:SEQ], ALU.mult), wait=False)
            step(g_.tensor_copy(sam[:, :, :, 0:2], halo[:].rearrange("p c (b j) -> p c b j", j=2)), wait=False)
            for c in range(NC):
                step(g_.tensor_tensor(sam[:, c, :, 2:], zs(ZGC)[:, c], zs(ZH)[:, c], ALU.mult))
            n = CL - 2
            for c in range(NC):
                cw = lambda j: vec[:, V_CW + 4 * j + c:V_CW + 4 * j + c + 1]
                step(g_.tensor_scalar(ca[:, c, 0:n], cu[:, c, 0:n], cw(0), None, ALU.mult))
                for j in (1, 2):
                    both(ca[:, c, 0:n], cu[:, c, j:n + j], cw(j), ca[:, c, 0:n], ALU.mult, ALU.add, ctmp[:, 0:n])
            cas = ca[:, :, SEQ + 2:CL].rearrange("p c (b s) -> p c b s", s=DEC_SEQ + 2)
            step(g_.tensor_tensor(z[:, ZH:ZH + NC, 0:SEQ], z[:, ZGB:ZGB + NC, 0:SEQ], ca[:, :, 0:SEQ], ALU.mult), wait=False)
            for c in range(NC):
                last = g_.tensor_tensor(zs(ZH)[:, c], zs(ZGB)[:, c], cas[:, c, :, 0:DEC_SEQ], ALU.mult)
                if c < NC - 1:
                    step(last)
            last.then_inc(S["conv_done"], 1)
            pool.wait_ge(S["unit_done"], SPL + N_IN)
            g_.memset(qst[:], 0.0).then_inc(S["q_zero"], 1)
            g_.tensor_copy(decay[:], arr(MAG)).then_inc(S["early_moved"], 1)
            g_.tensor_copy(base1[:], base1_made[:]).then_inc(S["early_moved"], 1)
            g_.tensor_copy(base16[:], base16_made[:]).then_inc(S["early_moved"], 1)
            pool.wait_ge(S["early_moved"], 3)
            step(g_.memset(us[:], 0.0))
            pool.wait_ge(S["bt_moved"], 2)
            pool.wait_ge(S["vp_moved"], 6)
            pool.wait_ge(S["kv_stored"], 32)
            pool.wait_ge(S["ssm_in"], 32)
            pool.wait_ge(S["c_ready"], 1)
            for x, one in ((tabc, 1.0), (tabs, 0.0)):
                for b in range(2):
                    step(g_.memset(x[:, b, SEQ:SL].rearrange("p (b s) -> p b s", s=STEP1)[:, :, 0:1], one))
            before = step.done
            with pool.Fori(0, NC) as it:
                step = Steps(pool, S["pool_step"])
                step.done = before
                step.enter(it, 44)

                def apart():
                    pool.wait_ge(S["kv_stored"], 32)

                def heads(r):
                    pool.wait_ge(S["po_done"], it * 4 + 2 * r + START)
                    apart()
                    for dst, t in ((qs, ZQ), (ks, ZK)):
                        step(g_.tensor_copy(dst[:].rearrange("p (a n) -> p a n", a=1), z[:, ds(it * 2 + (t + r), 1), 0:SEQ]), wait=False)
                    g_.tensor_copy(vs[:], vp[:, :, ds(it * (2 * P) + r * P, P)]).then_inc(S["q_static"], 1)

                def table(i):
                    b = i % 2
                    c_, s_ = tabc[:, b, :], tabs[:, b, :]
                    tile = ds(it * 4 + i, 1)
                    step(g_.tensor_copy(magc[:, b:b + 1], decay[:, tile]))
                    pool.wait_ge(S["ssm_h"], it * 4 + max(i - 1, 0) + START)
                    step(g_.tensor_tensor(dec[:, b, :], const[:, C_KEEP - P:C_END - P], magc[:, b:b + 1].to_broadcast([P, SL]), ALU.mult), wait=False)
                    near = [base1[:, j, tile, :].to_broadcast([P, TB, TB]) for j in range(2)]
                    far = [base16[:, j, tile, 0:TB].rearrange("p c (a b) -> p (c a) b", b=1).to_broadcast([P, TB, TB]) for j in range(2)]
                    cq, sq_, q0, q1 = (x.rearrange("p (a b) -> p a b", b=TB) for x in (c_[:, 0:SEQ], s_[:, 0:SEQ], ptmp[:, 0], ptmp[:, 1]))
                    step(g_.tensor_tensor(cq, far[0], near[0], ALU.mult), wait=False)
                    step(g_.tensor_tensor(sq_, far[1], near[0], ALU.mult), wait=False)
                    step(g_.tensor_tensor(q0, far[1], near[1], ALU.mult), wait=False)
                    step(g_.tensor_tensor(q1, far[0], near[1], ALU.mult), wait=False)
                    for j, x in enumerate((c_, s_)):
                        slots = x[:, SEQ:SL].rearrange("p (b s) -> p b s", s=STEP1)
                        step(g_.tensor_copy(slots[:, :, 1:], base1[:, j, tile, 0:DEC_SEQ].to_broadcast([P, DEC_BATCH, DEC_SEQ])), wait=j == 1)
                    step(g_.tensor_tensor(cq, cq, q0, ALU.subtract), wait=False)
                    g_.tensor_tensor(sq_, sq_, q1, ALU.add).then_inc(S["tab_ready"], 1)

                pool.wait_ge(S["y_acc"], it + START)
                apart()
                ub = z[:, ds(it + ZU, 1), :].rearrange("p a n -> p (a n)")
                step(g_.tensor_copy(us[:, 0:SEQ], ub[:, 0:SEQ]), wait=False)
                step(g_.tensor_copy(us[:, SEQ:SL].rearrange("p (b s) -> p b s", s=STEP1)[:, :, 1:],
                                    ub[:, SEQ:NT].rearrange("p (b s) -> p b s", s=DEC_SEQ)), wait=False)
                step(g_.tensor_copy(bs[:].rearrange("p a (c n) -> p a c n", c=1), bt[:, :, ds(it, 1), :]), wait=False)
                step(g_.tensor_copy(dcol[:], vec[:, ds(it + V_D, 1)]), wait=False)
                g_.tensor_copy(cs[:], cmat[:, :, ds(it * 4, 4), :]).then_inc(S["ssm_static"], 1)
                heads(0)
                table(0)
                table(1)
                heads(1)
                table(2)
                table(3)
                step.leave(NC)

        @block.tensor
        def _(pe):
            t_ = nc.tensor
            pe.sem_inc(S["unit_done"], SPL)
            pe.sem_inc(S["free0"], 1)
            pe.sem_inc(S["free1"], 1)
            pe.sem_inc(S["k_used"], 2)
            pe.sem_inc(S["v_used"], KEY_TILES)
            for name in ONE_AHEAD:
                pe.sem_inc(S[name], START)

            def sum_squares(k):
                first, n, _ = NORMS[k]
                src = sq_last if k == 5 else sq
                for i in range(n):
                    if i % 4 == 0:
                        pe.wait_ge(S["sq_ready"], tiles_before(k) // 4 + i // 4 + 1)
                    t_.matmul(ps[:, SUM_BANK[k], 0:NT], ones[:], src[:, first + i, :], start=(i == 0), stop=(i == n - 1)).then_inc(S["sq_used"], 1)

            def group(which, ah, al, it, g, ready=None, sums=None):
                _, first, _, units, before = GEMMS[which]
                pe.wait_ge(FREE[g], it + (before + 1))
                for j in range(units):
                    if sums and j == S3:
                        sum_squares(sums)
                    pe.wait_ge(S["w_lo"], it * (2 * units) + (RAW + first + g * units + j + 1))
                    slot = (g * units + j) % SPL
                    for kk in range(2):
                        k = 2 * j + kk
                        if ready is not None:
                            pe.wait_ge(S["m_lo"], ready + k + 1)
                        for n in range(4):
                            out = ps[:, 4 * g + n, 0:NT]
                            w = slice(512 * kk + P * n, 512 * kk + P * n + P)
                            t_.matmul(out, whi[:, slot, w], ah[:, k, :], start=(k == 0), stop=False)
                            t_.matmul(out, whi[:, slot, w], al[:, k, :], start=False, stop=False)
                            last = t_.matmul(out, wlo[:, slot, w], ah[:, k, :], start=False, stop=(k == 2 * units - 1))
                    last.then_inc(S["unit_done"], 1)

            def pairs(which, ah, al, start):
                with pe.Fori(start, GEMMS[which][2]) as it:
                    for g in range(2):
                        group(which, ah, al, it, g)

            def first_pair(which, k, ready):
                group(which, xh, xl, 0, 0, ready)
                pe.wait_ge(FREE[1], GEMMS[which][4] + 1)
                sum_squares(k)
                pe.wait_ge(S["var_ready"], k + 1)
                group(which, xh, xl, 0, 1)

            pe.wait_ge(S["ones_set"], 1)
            first_pair("in", 0, 0)
            pairs("in", xh, xl, 1)

            for g in range(2):
                pe.wait_ge(FREE[g], 1 + IN_COLS // 1024)
            pe.wait_ge(S["const_in"], 48)
            for c in range(6):
                cols = slice(P * (c // 2), P * (c // 2) + P) if c < 4 else slice(SEQ, NT)
                for i in range(4):
                    f = 4 * (c % 2) + i
                    last = t_.transpose(ps[0:(P if c < 4 else 64), c, P * i:P * i + P], z[:, ZV + f, cols], ident[:])
                last.then_inc(S["vpt_done"], 1)
            pe.wait_ge(S["bt_ready"], 2)
            for i in range(2):
                for c in range(NC):
                    last = t_.transpose(ps[:, 6 + i, P * c:P * c + P], bmat[:, i, 4 * c:4 * c + 4, :].rearrange("p s n -> p (s n)"), ident[:])
                last.then_inc(S["bt_done"], 1)
            pe.wait_ge(S["bt_moved"], 2)
            pe.wait_ge(S["vp_moved"], 6)

            with pe.Fori(0, NC) as it:
                def score_free(key):
                    n = score_turn[key] - 2
                    if n < 0:
                        pe.wait_ge(S["ps_masked"], it * 4 + START)
                        return
                    kind, r, g = next(k for k, m in score_turn.items() if m == n)
                    if kind == "s":
                        pe.wait_ge(S["s_masked"], it * 8 + (4 * r + (g + 1 if g < 2 else 4)))
                    else:
                        pe.wait_ge(S["ps_masked"], it * 4 + (2 * r + g + 1) + START)

                def turn_free(key):
                    n = turn[key] - 2
                    if n < 0:
                        pe.wait_ge(*((S["ppt_moved"], it * 4 + START) if n == -2 else (S["o_moved"], it * 8 + START)))
                        return
                    kind, r, g = next(k for k, m in turn.items() if m == n)
                    if kind == "pt":
                        pe.wait_ge(S["pt_moved"], it * 8 + (4 * r + (g + 1 if g < 2 else 4)))
                    elif kind == "pp":
                        pe.wait_ge(S["ppt_moved"], it * 4 + (2 * r + g + 1) + START)
                    else:
                        pe.wait_ge(S["o_moved"], it * 8 + (4 * r + 4) + START)

                def scores(r, g):
                    score_free(("s", r, g))
                    b = score_bank("s", r, g)
                    if g == 0:
                        pe.wait_ge(S["q_ready"], it * 8 + 4 * (r + 1))

                    def heads(cols, keys):
                        for i in range(2):
                            for c in range(4):
                                last = t_.matmul(ps[32 * c:32 * c + 32, b, cols], qst[:, r, 2 * c + i, :], keys(2 * c + i),
                                                 start=(i == 0), stop=(i == 1), tile_position=(0, 32 * c))
                        return last

                    if g == 2:
                        heads(slice(KU, KU + NT - SEQ), lambda f: z[:, ZK + f, SEQ:NT])
                    for u in range(2 * g, min(2 * g + 2, KN)):
                        n = KN * r + u
                        pe.wait_ge(K_IN[n % 2], it * (16 * KN) + 16 * (n // 2 + 1))
                        heads(slice(KU * (u - 2 * g), KU * (u - 2 * g) + KU), lambda f: kt[:, n % 2, f, :]).then_inc(S["k_used"], 1)

                def prompt_scores(r):
                    pe.wait_ge(S["q_static"], it * 2 + (r + 1))
                    for e in range(2):
                        score_free(("p", r, e))
                        b, h = score_bank("p", r, e), slice(64 * e, 64 * e + 64)
                        t_.matmul(ps[:, b, 0:P], qs[h, 0:P], ks[h, 0:P], start=True, stop=True)
                        t_.matmul(ps[:, b, P:3 * P], qs[h, P:2 * P], ks[h, :], start=True, stop=True).then_inc(S["ps_done"], 1)

                def probabilities(r):
                    pe.wait_ge(S["p_exp"], it * 2 + (r + 1))
                    for g in range(3):
                        turn_free(("pt", r, g))
                        b = turn_bank("pt", r, g)
                        for i in range(4 if g < 2 else 2):
                            n = 4 * g + i
                            last = t_.transpose(ps[:, b, P * i:P * i + P], sall[:, P * n:P * n + P], ident[:])
                        if g == 2:
                            last = t_.transpose(ps[0:64, b, 256:384], sall[:, KEY_TILES * P:NKEYS], ident[:])
                        last.then_inc(S["pt_done"], 1)
                    pe.wait_ge(S["po_moved"], it * 2 + r + START)
                    for j in range(KEY_TILES + 1):
                        if j % 4 == 0:
                            pe.wait_ge(S["pt_moved"], it * 8 + (4 * r + (j // 4 + 1 if j < 8 else 4)))
                        if j < KEY_TILES:
                            pe.wait_ge(V_IN[j], it * 32 + 16 * (r + 1))
                        for c in range(4):
                            rows, w = slice(0, P if j < KEY_TILES else 64), slice(2 * P * c, 2 * P * c + 2 * P)
                            vals = vt[:, j, w] if j < KEY_TILES else vn[0:64, w]
                            last = t_.matmul(ps[32 * c:32 * c + 32, 4, 0:2 * P], ptk[rows, j, 32 * c:32 * c + 32], vals,
                                             start=(j == 0), stop=(j == KEY_TILES), tile_position=(0, 32 * c))
                        last.then_inc(S["v_used"] if j < KEY_TILES else S["o_done"], 1)

                def turn_output(r):
                    pe.wait_ge(S["o_scaled"], it * 2 + (r + 1) + START)
                    turn_free(("o", r, 0))
                    for i in range(2):
                        last = t_.transpose(ps[:, turn_bank("o", r, 0), P * i:P * i + P], osb[:, P * i:P * i + P], ident[:])
                    last.then_inc(S["o_turned"], 1)

                def turn_prompt(r):
                    for e in range(2):
                        pe.wait_ge(S["pp_norm"], it * 4 + (2 * r + e + 1))
                        turn_free(("pp", r, e))
                        b = turn_bank("pp", r, e)
                        for i in range(3):
                            last = t_.transpose(ps[:, b, P * i:P * i + P], sp[:, e, P * i:P * i + P], ident[:])
                        last.then_inc(S["ppt_done"], 1)

                def prompt_output(r):
                    for e in range(2):
                        pe.wait_ge(S["ppt_moved"], it * 4 + (2 * r + e + 1) + START)
                        h = slice(64 * e, 64 * e + 64)
                        t_.matmul(ps[h, 4, 0:P], vs[:, 0, h], ptp[:, e, 0:P], start=True, stop=True)
                        t_.matmul(ps[h, 4, P:SEQ], vs[:, 0, h], ptp[:, e, P:SEQ], start=True, stop=False)
                        t_.matmul(ps[h, 4, P:SEQ], vs[:, 1, h], ptp[:, e, SEQ:3 * P], start=False, stop=True) \
                            .then_inc(S["po_done"], 1)

                def project(i):
                    if i == 0:
                        pe.wait_ge(S["ssm_static"], it + 1)
                    pe.wait_ge(S["x_rot"], it * 4 + i + START)
                    q = slice(32 * i, 32 * i + 32)
                    t_.matmul(ps[:, 6, 0:SL], bs[q, 0, :], us[q, :], start=True, stop=True, tile_position=(32 * i, 0))
                    t_.matmul(ps[:, 7, 0:SL], bs[q, 1, :], us[q, :], start=True, stop=True, tile_position=(32 * i, 0)).then_inc(S["x_proj"], 1)

                def read_out(i):
                    pe.wait_ge(S["ssm_h"], it * 4 + (i + 1) + START)
                    if i == 0:
                        pe.wait_ge(S["y_acc"], it + START)
                    q = slice(32 * i, 32 * i + 32)
                    t_.matmul(ps[q, 5, 0:SL], cs[:, 0, i, :], hb[:, i % 2, 0], start=True, stop=False)
                    t_.matmul(ps[q, 5, 0:SL], cs[:, 1, i, :], hb[:, i % 2, 1], start=False, stop=True).then_inc(S["c_done"], 1)

                for r in range(2):
                    for g in range(3):
                        scores(r, g)
                    prompt_scores(r)
                    project(2 * r)
                    if r:
                        read_out(1)
                    probabilities(r)
                    turn_prompt(r)
                    project(2 * r + 1)
                    turn_output(r)
                    prompt_output(r)
                    read_out(2 * r)
                read_out(3)

            pe.wait_ge(S["po_moved"], 2 * NC + START)
            pe.wait_ge(S["o_moved"], 8 * NC + START)
            pe.wait_ge(S["y_acc"], NC + START)
            sum_squares(1)
            sum_squares(2)
            pe.wait_ge(S["glu_in"], 16)
            pe.wait_ge(S["y_glu"], NC)
            for n in range(NC):
                for k in range(NC):
                    last = t_.matmul(ps[:, n, 0:NT], wglu[:, k, P * n:P * n + P], z[:, ZU + k, :], start=(k == 0), stop=(k == NC - 1))
                last.then_inc(S["glu_done"], 1)
            pe.wait_ge(S["glu_sig"], NC)
            group("out", hh, hl, 0, 0, KT, 3)
            group("out", hh, hl, 0, 1)
            pairs("out", hh, hl, 1)
            first_pair("gu", 4, 2 * KT)
            pairs("gu", xh, xl, 1)
            pe.wait_ge(S["h_lo"], D_FF // 512)
            pairs("dn", hh, hl, 0)
            pe.wait_ge(FREE[0], 1 + PAIRS)
            sum_squares(5)


def pack_weights(w):
    k, n = w.shape
    return np.ascontiguousarray(w.reshape(k // 256, 2, P, n // 512, 512).transpose(3, 0, 2, 1, 4)).reshape(-1, P, UNIT)


def features(x):
    return x.reshape(x.shape[0], -1, P).transpose(2, 1, 0)


def kernel(x_prompt, x_sample, cache_kv, state_conv, state_ssm_re, state_ssm_im, g_mix_norm, w_in, ssm_a_re, ssm_a_im,
           ssm_log_dt, ssm_b_re, ssm_b_im, ssm_c_re, ssm_c_im, ssm_d, ssm_w_glu, ssm_b_glu, conv_w, g_out, w_out,
           g_ffn_norm, w_gate, w_up, w_down, g_final):
    import concourse.bacc as bacc
    from concourse.bass_utils import run_bass_kernel_spmd

    arr = np.asarray
    ins = {}
    ins["xt"] = np.concatenate([features(arr(x_prompt)[0]), features(arr(x_sample).reshape(-1, D_MODEL))], axis=2)
    pos = cache_positions()
    kv = arr(cache_kv)[0]
    ck = kv[:, pos, 0].reshape(DEC_BATCH, KN, KU, NF, P)
    ins["ck"] = ck.transpose(0, 1, 4, 3, 2).reshape(-1, P, NF * KU)
    ins["cv"] = kv[:, pos, 1].reshape(-1, P, ATT_WIDTH)
    U0 = 3 * ATT_WIDTH
    ins["w_in"] = pack_weights(arr(w_in)[0][:, np.r_[U0 + SSM_WIDTH:IN_COLS, U0:U0 + SSM_WIDTH, 0:U0]])
    done = np.r_[ATT_WIDTH + SSM_WIDTH:D_MODEL, 0:ATT_WIDTH + SSM_WIDTH]
    ins["w_out"] = pack_weights(arr(w_out)[0][done])
    gate, up = pack_weights(arr(w_gate)[0]), pack_weights(arr(w_up)[0])
    ins["w_gu"] = np.stack([x.reshape(-1, U_IN, P, UNIT) for x in (gate, up)], axis=1).reshape(-1, P, UNIT)
    ins["w_dn"] = pack_weights(arr(w_down)[0])
    col = lambda x: arr(x).reshape(-1, P).T
    states = lambda x: arr(x).reshape(ST, P).T
    dt = np.repeat(arr(ssm_log_dt)[0], SSM_STATE)
    ins["vecs"] = np.concatenate([col(g_mix_norm), col(arr(g_out)[0][done]), col(g_ffn_norm), col(g_final), col(ssm_d), col(ssm_b_glu),
                                  col(conv_w), states(ssm_a_re), states(ssm_a_im), states(dt)], axis=1)
    ins["halo"] = features(arr(state_conv)[0].reshape(-1, CONV_CH))
    ins["state"] = np.stack([arr(x)[0].reshape(DEC_BATCH, ST, P).transpose(2, 1, 0) for x in (state_ssm_re, state_ssm_im)], axis=1)

    def blocks(x):
        x = x.reshape(ST, 2, SSM_STATE, SSM_GROUP)
        out = np.zeros((ST, 2, SSM_STATE, 2, SSM_GROUP), x.dtype)
        out[:, 0, :, 0], out[:, 1, :, 1] = x[:, 0], x[:, 1]
        return out.reshape(ST, P, 32).transpose(1, 0, 2)

    ins["ssm_b"] = np.stack([blocks(arr(x)[0]) for x in (ssm_b_re, ssm_b_im)], axis=1)
    ins["ssm_c"] = np.stack([blocks(arr(x)[0].transpose(0, 2, 1)) for x in (ssm_c_re, ssm_c_im)], axis=1)
    ins["w_glu"] = arr(ssm_w_glu)[0].reshape(NC, P, SSM_WIDTH).transpose(1, 0, 2)
    ins["consts"] = constants()

    outs = {"y": (P, KT, NT), "kv": (P, 2 * NF, NT), "conv": (P, NC, 2 + 2 * DEC_BATCH), "state": (P, 2, ST, STEP1)}
    nc = bacc.Bacc("TRN2", target_bir_lowering=False, num_devices=1)
    arrays, a, o = {}, {}, {}
    for name, x in ins.items():
        x = np.ascontiguousarray(x)
        arrays[f"in_{name}"] = x
        a[name] = nc.dram_tensor(f"in_{name}", x.shape, mybir.dt.from_np(x.dtype), kind="ExternalInput").ap()
    for name, shape in outs.items():
        o[name] = nc.dram_tensor(f"out_{name}", shape, F32, kind="ExternalOutput").ap()
    build(nc, a, o)
    got = run_bass_kernel_spmd(nc, [arrays], core_ids=[0]).results[0]

    def tokens(x):
        return arr(x).transpose(2, 1, 0).reshape(x.shape[2], -1)

    y, kvt = tokens(got["out_y"]), got["out_kv"]
    kvt = np.stack([tokens(kvt[:, :NF]), tokens(kvt[:, NF:])], axis=1).reshape(NT, 2, N_HEADS, HEAD_DIM)
    conv = tokens(got["out_conv"])
    st = arr(got["out_state"]).transpose(1, 3, 2, 0).reshape(2, STEP1, N_GROUPS, SSM_STATE)
    c = np.ascontiguousarray
    return (c(y[:SEQ][None]), c(y[SEQ:].reshape(DEC_BATCH, DEC_SEQ, D_MODEL)),
            c(kvt[:SEQ][None, None]), c(conv[:2][None, None]), c(st[0, 0][None, None]), c(st[1, 0][None, None]),
            c(kvt[SEQ:].reshape(1, DEC_BATCH, DEC_SEQ, 2, N_HEADS, HEAD_DIM)),
            c(conv[2:].reshape(1, DEC_BATCH, 2, CONV_CH)), c(st[0, 1:][None]), c(st[1, 1:][None]))
```
